# Optimizing a Trainium2 kernel written in Bass

```python
import math
import jax, jax.numpy as jnp
from jax import lax
import numpy as np

D_MODEL = 1024
BATCH = 1
SEQ = 1024
DEPTH = 2
DEC_BATCH = 8
DEC_SEQ = 16
PAST_LEN = 1024

CHUNK = 64
N_EVEN = (DEPTH + 1) // 2
N_ODD = DEPTH // 2
EPS = 1e-6
CONV_W = 4
NEG_INF = -1e30
LRU_WIDTH = D_MODEL // 2
LRU_HEADS = 8
LRU_BLOCK = LRU_WIDTH // LRU_HEADS
LRU_C = 8.0
HEAD_DIM = 64
ATT_HEADS = (D_MODEL // 2) // HEAD_DIM
ATT_KV_HEADS = 2
ATT_GROUP = ATT_HEADS // ATT_KV_HEADS
WINDOW = 128
ROT_DIM = HEAD_DIM // 4
ROPE_THETA = 500000.0
ATT_WIDTH = ATT_HEADS * HEAD_DIM
KV_WIDTH = ATT_KV_HEADS * HEAD_DIM
EVEN_IN = 2 * LRU_WIDTH + ATT_WIDTH + 2 * KV_WIDTH + ATT_WIDTH
EVEN_MIX = LRU_WIDTH + ATT_WIDTH
EVEN_SPLITS = (LRU_WIDTH, 2 * LRU_WIDTH, 2 * LRU_WIDTH + ATT_WIDTH,
               2 * LRU_WIDTH + ATT_WIDTH + KV_WIDTH, 2 * LRU_WIDTH + ATT_WIDTH + 2 * KV_WIDTH)
GDN_DK = 128
GDN_DV = 128
GDN_HEADS = D_MODEL // GDN_DV
GDN_KW = GDN_HEADS * GDN_DK
GDN_VW = GDN_HEADS * GDN_DV
GDN_CONV_CH = 2 * GDN_KW + GDN_VW
ODD_IN = GDN_CONV_CH + GDN_VW + 2 * GDN_HEADS
ODD_SPLITS = (GDN_CONV_CH, GDN_CONV_CH + GDN_VW, GDN_CONV_CH + GDN_VW + GDN_HEADS)

kernel_name = "hybrid_streaming_encoder_step"

def rms_norm(x, g):
    xf = x.astype(jnp.float32)
    y = xf * lax.rsqrt(jnp.mean(xf * xf, axis=-1, keepdims=True) + EPS)
    return (y * g.astype(jnp.float32)).astype(x.dtype)

def l2_normalize(x):
    return x * lax.rsqrt(jnp.sum(x * x, axis=-1, keepdims=True) + EPS)

def modulate(c, mod_w, mod_b):
    mod = jnp.dot(jax.nn.silu(c), mod_w) + mod_b
    shift, scale, gate = jnp.split(mod, 3, axis=-1)
    return shift[:, None], scale[:, None], gate[:, None]

def causal_dwconv(u, buf, w):
    t = u.shape[1]
    ext = jnp.concatenate([buf.astype(u.dtype), u], axis=1)
    y = ext[:, 0:t] * w[0]
    for j in range(1, CONV_W):
        y = y + ext[:, j:j + t] * w[j]
    return y, ext[:, t:]

def partial_rope(x, pos):
    half = ROT_DIM // 2
    inv = ROPE_THETA ** (-(jnp.arange(half, dtype=jnp.float32) * 2.0 / ROT_DIM))
    ang = pos.astype(jnp.float32)[:, None] * inv[None, :]
    cos = jnp.cos(ang)[None, :, None, :]
    sin = jnp.sin(ang)[None, :, None, :]
    xf = x.astype(jnp.float32)
    x1 = xf[..., :half]
    x2 = xf[..., half:ROT_DIM]
    out = jnp.concatenate([x1 * cos - x2 * sin, x2 * cos + x1 * sin, xf[..., ROT_DIM:]], axis=-1)
    return out.astype(x.dtype)

def rg_lru(x, h0, w_a, b_a, w_x, b_x, lam):
    bsz, t, _ = x.shape
    xf = x.astype(jnp.float32)
    xb = xf.reshape(bsz, t, LRU_HEADS, LRU_BLOCK)
    r = jax.nn.sigmoid(jnp.einsum('bthi,hij->bthj', xb, w_a.astype(jnp.float32)).reshape(bsz, t, LRU_WIDTH) + b_a)
    i = jax.nn.sigmoid(jnp.einsum('bthi,hij->bthj', xb, w_x.astype(jnp.float32)).reshape(bsz, t, LRU_WIDTH) + b_x)
    log_a = -LRU_C * r * jax.nn.softplus(-lam.astype(jnp.float32))
    a = jnp.exp(log_a)
    gated_x = jnp.sqrt(-jnp.expm1(2.0 * log_a)) * (i * xf)

    def combine(lhs, rhs):
        a_l, b_l = lhs
        a_r, b_r = rhs
        return a_l * a_r, a_r * b_l + b_r

    a_cum, h_zero = lax.associative_scan(combine, (a, gated_x), axis=1)
    h = h_zero + a_cum * h0.astype(jnp.float32)[:, None]
    return h.astype(x.dtype), h[:, -1].astype(x.dtype)

def sink_window_attention(q, k, v, k_past, v_past, n_past_valid, sinks):
    bsz, t = q.shape[:2]
    cb = min(CHUNK, t)
    nb = t // cb
    m = WINDOW + cb
    k_ext = jnp.concatenate([k_past.astype(k.dtype), k], axis=1)
    v_ext = jnp.concatenate([v_past.astype(v.dtype), v], axis=1)
    idx = jnp.arange(nb)[:, None] * cb + jnp.arange(m)[None, :]
    kb = jnp.take(k_ext, idx, axis=1)
    vb = jnp.take(v_ext, idx, axis=1)
    qb = q.reshape(bsz, nb, cb, ATT_KV_HEADS, ATT_GROUP, HEAD_DIM)
    s = jnp.einsum('bnqhgd,bnmhd->bnhgqm', qb, kb,
                   preferred_element_type=jnp.float32) * (HEAD_DIM ** -0.5)
    valid = idx >= (WINDOW - n_past_valid)
    s = jnp.where(valid[None, :, None, None, None, :], s, NEG_INF)
    sink = sinks.astype(jnp.float32).reshape(ATT_KV_HEADS, ATT_GROUP)[None, None, :, :, None, None]
    mx = jnp.maximum(jnp.max(s, axis=-1, keepdims=True), sink)
    p = jnp.exp(s - mx)
    p = p / (jnp.sum(p, axis=-1, keepdims=True) + jnp.exp(sink - mx))
    o = jnp.einsum('bnhgqm,bnmhd->bnqhgd', p.astype(v.dtype), vb)
    return o.reshape(bsz, t, ATT_WIDTH)

def unit_lower_inverse(a, n):
    t = jnp.broadcast_to(jnp.eye(n, dtype=a.dtype), a.shape)
    p = -a
    n_steps = (n - 1).bit_length()
    for step in range(n_steps):
        t = t + jnp.matmul(t, p)
        if step + 1 < n_steps:
            p = jnp.matmul(p, p)
    return t

def gated_delta_rule(q, k, v, g, beta, s0):
    bsz, t, h, _ = q.shape
    dv = v.shape[-1]
    cb = min(CHUNK, t)
    nc = t // cb

    def chunks(a):
        a = a.reshape(bsz, nc, cb, h, -1)
        return jnp.transpose(a, (1, 0, 3, 2, 4))

    qc, kc, vc = chunks(q), chunks(k), chunks(v)
    gc = chunks(g[..., None])[..., 0]
    bc = chunks(beta[..., None])[..., 0]
    gcum = jnp.cumsum(gc, axis=-1)
    strict = jnp.tril(jnp.ones((cb, cb), dtype=bool), -1)
    incl = jnp.tril(jnp.ones((cb, cb), dtype=bool))
    diff = gcum[..., :, None] - gcum[..., None, :]
    decay_strict = jnp.where(strict, jnp.exp(jnp.where(strict, diff, 0.0)), 0.0)
    decay_incl = jnp.where(incl, jnp.exp(jnp.where(incl, diff, 0.0)), 0.0)
    k_beta = kc * bc[..., None]
    a_mat = jnp.einsum('nbhid,nbhjd->nbhij', k_beta, kc) * decay_strict
    t_mat = unit_lower_inverse(a_mat, cb)
    w = jnp.matmul(t_mat, k_beta * jnp.exp(gcum)[..., None])
    u = jnp.matmul(t_mat, vc * bc[..., None])
    qk = jnp.einsum('nbhid,nbhjd->nbhij', qc, kc) * decay_incl

    def step(state, inp):
        q_i, k_i, w_i, u_i, qk_i, g_i = inp
        v_new = u_i - jnp.einsum('bhck,bhkv->bhcv', w_i, state)
        o_i = (jnp.einsum('bhck,bhkv->bhcv', q_i * jnp.exp(g_i)[..., None], state)
               + jnp.einsum('bhcj,bhjv->bhcv', qk_i, v_new))
        g_last = g_i[..., -1:]
        k_dec = k_i * jnp.exp(g_last - g_i)[..., None]
        state = state * jnp.exp(g_last)[..., None] + jnp.einsum('bhck,bhcv->bhkv', k_dec, v_new)
        return state, o_i

    s_final, o = lax.scan(step, s0, (qc, kc, w, u, qk, gcum))
    o = jnp.transpose(o, (1, 0, 3, 2, 4)).reshape(bsz, t, h, dv)
    return o, s_final

def even_layer(x, c, conv_buf, h0, k_past, v_past, n_past_valid, pos0,
               mod_w, mod_b, norm_pre, norm_post, w_in, conv_w, conv_b,
               w_a, b_a, w_x, b_x, lam, sinks, w_out):
    bsz, t, _ = x.shape
    shift, scale, gate = modulate(c, mod_w, mod_b)
    hmod = rms_norm(x, norm_pre) * (1.0 + scale) + shift
    u = jnp.dot(hmod, w_in)
    x_a, g_a, q, k, v, g_b = jnp.split(u, EVEN_SPLITS, axis=-1)
    xc, new_buf = causal_dwconv(x_a, conv_buf, conv_w)
    h, h_last = rg_lru(xc + conv_b, h0, w_a, b_a, w_x, b_x, lam)
    y_a = h * jax.nn.silu(g_a)
    pos = pos0 + jnp.arange(t, dtype=jnp.int32)
    q = partial_rope(q.reshape(bsz, t, ATT_HEADS, HEAD_DIM), pos)
    k = partial_rope(k.reshape(bsz, t, ATT_KV_HEADS, HEAD_DIM), pos)
    v = v.reshape(bsz, t, ATT_KV_HEADS, HEAD_DIM)
    y_b = sink_window_attention(q, k, v, k_past, v_past, n_past_valid, sinks) * jax.nn.silu(g_b)
    y = jnp.dot(jnp.concatenate([y_a, y_b], axis=-1), w_out)
    x = x + gate * rms_norm(y, norm_post)
    return x, new_buf, h_last, k, v

def odd_layer(x, c, conv_buf, s0, mod_w, mod_b, norm_pre, norm_post, w_in,
              conv_w, a_log, dt_bias, head_norm, w_out):
    bsz, t, _ = x.shape
    shift, scale, gate = modulate(c, mod_w, mod_b)
    hmod = rms_norm(x, norm_pre) * (1.0 + scale) + shift
    u = jnp.dot(hmod, w_in)
    qkv, z, b, a = jnp.split(u, ODD_SPLITS, axis=-1)
    qkv_c, new_buf = causal_dwconv(qkv, conv_buf, conv_w)
    qkv_c = jax.nn.silu(qkv_c).astype(jnp.float32)
    q, k, v = jnp.split(qkv_c, (GDN_KW, 2 * GDN_KW), axis=-1)
    q = l2_normalize(q.reshape(bsz, t, GDN_HEADS, GDN_DK)) * (GDN_DK ** -0.5)
    k = l2_normalize(k.reshape(bsz, t, GDN_HEADS, GDN_DK))
    v = v.reshape(bsz, t, GDN_HEADS, GDN_DV)
    beta = jax.nn.sigmoid(b.astype(jnp.float32))
    g = -jnp.exp(a_log.astype(jnp.float32)) * jax.nn.softplus(a.astype(jnp.float32) + dt_bias)
    o, s_new = gated_delta_rule(q, k, v, g, beta, s0.astype(jnp.float32))
    o = rms_norm(o, head_norm) * jax.nn.silu(z.reshape(bsz, t, GDN_HEADS, GDN_DV).astype(jnp.float32))
    y = jnp.dot(o.reshape(bsz, t, GDN_VW).astype(x.dtype), w_out)
    x = x + gate * rms_norm(y, norm_post)
    return x, new_buf, s_new.astype(x.dtype)

def setup_inputs(seed: int = 0) -> dict:
    key = jax.random.key(seed)
    ks = iter(jax.random.split(key, 48))
    f32 = jnp.float32

    def nrm(shape, scale):
        return jax.random.normal(next(ks), shape, f32) * scale

    x_prompt = nrm((BATCH, SEQ, D_MODEL), 1.0)
    x_sample = nrm((DEC_BATCH, DEC_SEQ, D_MODEL), 1.0)
    state_lru_conv = nrm((N_EVEN, DEC_BATCH, CONV_W - 1, LRU_WIDTH), 1.0)
    state_lru_h = nrm((N_EVEN, DEC_BATCH, LRU_WIDTH), 0.5)
    cache_swa_k = nrm((N_EVEN, DEC_BATCH, WINDOW, ATT_KV_HEADS, HEAD_DIM), 1.0)
    cache_swa_v = nrm((N_EVEN, DEC_BATCH, WINDOW, ATT_KV_HEADS, HEAD_DIM), 1.0)
    state_gdn_conv = nrm((N_ODD, DEC_BATCH, CONV_W - 1, GDN_CONV_CH), 1.0)
    state_gdn_s = nrm((N_ODD, DEC_BATCH, GDN_HEADS, GDN_DK, GDN_DV), GDN_DK ** -0.5)
    c_prompt = nrm((BATCH, D_MODEL), 1.0)
    c_sample = nrm((DEC_BATCH, D_MODEL), 1.0)
    ev_mod_w = nrm((N_EVEN, D_MODEL, 3 * D_MODEL), 0.2 * D_MODEL ** -0.5)
    ev_mod_b = nrm((N_EVEN, 3 * D_MODEL), 0.02)
    ev_norm_pre = 1.0 + nrm((N_EVEN, D_MODEL), 0.02)
    ev_norm_post = 1.0 + nrm((N_EVEN, D_MODEL), 0.02)
    ev_w_in = nrm((N_EVEN, D_MODEL, EVEN_IN), D_MODEL ** -0.5)
    lru_conv_w = nrm((N_EVEN, CONV_W, LRU_WIDTH), CONV_W ** -0.5)
    lru_conv_b = nrm((N_EVEN, LRU_WIDTH), 0.02)
    lru_w_a = nrm((N_EVEN, LRU_HEADS, LRU_BLOCK, LRU_BLOCK), LRU_BLOCK ** -0.5)
    lru_b_a = nrm((N_EVEN, LRU_WIDTH), 0.02)
    lru_w_x = nrm((N_EVEN, LRU_HEADS, LRU_BLOCK, LRU_BLOCK), LRU_BLOCK ** -0.5)
    lru_b_x = nrm((N_EVEN, LRU_WIDTH), 0.02)
    u_lam = jax.random.uniform(next(ks), (N_EVEN, LRU_WIDTH), f32, 0.9, 0.999)
    lru_lambda = jnp.log(u_lam) - jnp.log1p(-u_lam)
    swa_sinks = nrm((N_EVEN, ATT_HEADS), 1.0)
    ev_w_out = nrm((N_EVEN, EVEN_MIX, D_MODEL), EVEN_MIX ** -0.5)
    od_mod_w = nrm((N_ODD, D_MODEL, 3 * D_MODEL), 0.2 * D_MODEL ** -0.5)
    od_mod_b = nrm((N_ODD, 3 * D_MODEL), 0.02)
    od_norm_pre = 1.0 + nrm((N_ODD, D_MODEL), 0.02)
    od_norm_post = 1.0 + nrm((N_ODD, D_MODEL), 0.02)
    od_w_in = nrm((N_ODD, D_MODEL, ODD_IN), D_MODEL ** -0.5)
    gdn_conv_w = nrm((N_ODD, CONV_W, GDN_CONV_CH), CONV_W ** -0.5)
    gdn_a_log = jnp.log(jax.random.uniform(next(ks), (N_ODD, GDN_HEADS), f32, 1.0, 16.0))
    dt = jnp.exp(jax.random.uniform(next(ks), (N_ODD, GDN_HEADS), f32, math.log(1e-3), math.log(1e-1)))
    gdn_dt_bias = dt + jnp.log(-jnp.expm1(-dt))
    gdn_head_norm = 1.0 + nrm((N_ODD, GDN_DV), 0.02)
    od_w_out = nrm((N_ODD, GDN_VW, D_MODEL), GDN_VW ** -0.5)
    return {
        'x_prompt': x_prompt, 'x_sample': x_sample,
        'state_lru_conv': state_lru_conv, 'state_lru_h': state_lru_h,
        'cache_swa_k': cache_swa_k, 'cache_swa_v': cache_swa_v,
        'state_gdn_conv': state_gdn_conv, 'state_gdn_s': state_gdn_s,
        'c_prompt': c_prompt, 'c_sample': c_sample,
        'ev_mod_w': ev_mod_w, 'ev_mod_b': ev_mod_b, 'ev_norm_pre': ev_norm_pre, 'ev_norm_post': ev_norm_post,
        'ev_w_in': ev_w_in, 'lru_conv_w': lru_conv_w, 'lru_conv_b': lru_conv_b,
        'lru_w_a': lru_w_a, 'lru_b_a': lru_b_a, 'lru_w_x': lru_w_x, 'lru_b_x': lru_b_x,
        'lru_lambda': lru_lambda, 'swa_sinks': swa_sinks, 'ev_w_out': ev_w_out,
        'od_mod_w': od_mod_w, 'od_mod_b': od_mod_b, 'od_norm_pre': od_norm_pre, 'od_norm_post': od_norm_post,
        'od_w_in': od_w_in, 'gdn_conv_w': gdn_conv_w, 'gdn_a_log': gdn_a_log, 'gdn_dt_bias': gdn_dt_bias,
        'gdn_head_norm': gdn_head_norm, 'od_w_out': od_w_out,
    }

def reference(x_prompt, x_sample, state_lru_conv, state_lru_h, cache_swa_k, cache_swa_v,
              state_gdn_conv, state_gdn_s, c_prompt, c_sample,
              ev_mod_w, ev_mod_b, ev_norm_pre, ev_norm_post, ev_w_in, lru_conv_w, lru_conv_b,
              lru_w_a, lru_b_a, lru_w_x, lru_b_x, lru_lambda, swa_sinks, ev_w_out,
              od_mod_w, od_mod_b, od_norm_pre, od_norm_post, od_w_in, gdn_conv_w, gdn_a_log,
              gdn_dt_bias, gdn_head_norm, od_w_out):
    xp, xs = x_prompt, x_sample
    bp = xp.shape[0]
    lru_conv_p, lru_conv_s, lru_h_p, lru_h_s = [], [], [], []
    swa_k_p, swa_k_s, swa_v_p, swa_v_s = [], [], [], []
    gdn_conv_p, gdn_conv_s, gdn_s_p, gdn_s_s = [], [], [], []
    for layer in range(DEPTH):
        if layer % 2 == 0:
            e = layer // 2
            ew = (ev_mod_w[e], ev_mod_b[e], ev_norm_pre[e], ev_norm_post[e], ev_w_in[e],
                  lru_conv_w[e], lru_conv_b[e], lru_w_a[e], lru_b_a[e], lru_w_x[e], lru_b_x[e],
                  lru_lambda[e], swa_sinks[e], ev_w_out[e])
            zero_buf = jnp.zeros((bp, CONV_W - 1, LRU_WIDTH), xp.dtype)
            zero_h = jnp.zeros((bp, LRU_WIDTH), xp.dtype)
            zero_kv = jnp.zeros((bp, WINDOW, ATT_KV_HEADS, HEAD_DIM), xp.dtype)
            xp, buf_p, h_p, k_p, v_p = even_layer(xp, c_prompt, zero_buf, zero_h, zero_kv, zero_kv, 0, 0, *ew)
            xs, buf_s, h_s, k_s, v_s = even_layer(xs, c_sample, state_lru_conv[e], state_lru_h[e],
                                                  cache_swa_k[e], cache_swa_v[e], WINDOW, PAST_LEN, *ew)
            lru_conv_p.append(buf_p)
            lru_conv_s.append(buf_s)
            lru_h_p.append(h_p)
            lru_h_s.append(h_s)
            swa_k_p.append(k_p[:, -WINDOW:])
            swa_v_p.append(v_p[:, -WINDOW:])
            swa_k_s.append(k_s)
            swa_v_s.append(v_s)
        else:
            o = layer // 2
            ow = (od_mod_w[o], od_mod_b[o], od_norm_pre[o], od_norm_post[o], od_w_in[o],
                  gdn_conv_w[o], gdn_a_log[o], gdn_dt_bias[o], gdn_head_norm[o], od_w_out[o])
            zero_buf = jnp.zeros((bp, CONV_W - 1, GDN_CONV_CH), xp.dtype)
            zero_s = jnp.zeros((bp, GDN_HEADS, GDN_DK, GDN_DV), jnp.float32)
            xp, buf_p, st_p = odd_layer(xp, c_prompt, zero_buf, zero_s, *ow)
            xs, buf_s, st_s = odd_layer(xs, c_sample, state_gdn_conv[o], state_gdn_s[o], *ow)
            gdn_conv_p.append(buf_p)
            gdn_conv_s.append(buf_s)
            gdn_s_p.append(st_p)
            gdn_s_s.append(st_s)
    return (xp, xs,
            jnp.stack(lru_conv_p), jnp.stack(lru_conv_s),
            jnp.stack(lru_h_p), jnp.stack(lru_h_s),
            jnp.stack(swa_k_p), jnp.stack(swa_k_s),
            jnp.stack(swa_v_p), jnp.stack(swa_v_s),
            jnp.stack(gdn_conv_p), jnp.stack(gdn_conv_s),
            jnp.stack(gdn_s_p), jnp.stack(gdn_s_s))


_drawn_inputs = setup_inputs


def setup_inputs(seed=0):
    import zlib

    import numpy as np

    out = dict(_drawn_inputs(seed))
    spreads = {}
    factors = {'ev_norm_pre': 2.755,
     'ev_norm_post': 8.0,
     'lru_b_a': 8.0,
     'lru_b_x': 7.57,
     'swa_sinks': 8.0,
     'od_norm_post': 8.0,
     'gdn_head_norm': 8.0}
    for name, (base, spread) in spreads.items():
        noise = np.random.default_rng([zlib.crc32(name.encode()), seed]).standard_normal(out[name].shape)
        drawn = base * np.exp(spread * noise) if base else spread * noise
        out[name] = __import__('jax').numpy.asarray(drawn.astype(out[name].dtype))
    for name, factor in factors.items():
        out[name] = (out[name] * factor).astype(out[name].dtype)
    return out
```

```python
from contextlib import ExitStack

import numpy as np
import concourse.bass as bass
from concourse import mybir

F32 = mybir.dt.float32
ALU = mybir.AluOpType
ACT = mybir.ActivationFunctionType
AX = mybir.AxisListType

P = 128
D = 1024
KT = D // P
SEQ, NS, DS = 1024, 8, 16
NT = SEQ // P + 1
TOK = NT * P
NC = TOK // 3
LW = 512
LM = LW // P
H = 8
HD = 64
TAPS = 4
PRE = TAPS - 1
UW = PRE + SEQ + NS * (PRE + DS)
UC = UW - PRE
US = PRE + SEQ
EPS = 1e-6
NEG = -1e30
WIN = 128


def wait(eng, sem, value):
    eng.wait_ge(sem, value)
    if not isinstance(value, int):
        eng.sem_inc(PASSED[eng.engine], 1)


PASSED = {}

GROUPS, GB = 12, 9


def _places():
    plan = []
    for batches, levels, steps, lo, hi in ((2, 6, 12, 0, 8 * GB), (1, 3, 4, 8 * GB, 8 * GROUPS)):
        weights = ([3, 2, 3] + [1] * (3 * levels - (levels == 6)) + [1] * steps + [1, 1]) * batches
        ends = [lo + (hi - lo) * sum(weights[:i + 1]) // sum(weights) for i in range(len(weights))]
        spans = list(zip([lo] + ends, ends))
        n = len(spans) // batches
        plan += [spans[i * n:(i + 1) * n] for i in range(batches)]
    return plan


PLACES = _places()


def ended(b, place):
    lo, hi = PLACES[b][place]
    return [g for g in range(GROUPS) if lo < 8 * g + 8 <= hi]


def ended_before(b, place, back):
    while place < back:
        if b == 0:
            return []
        b -= 1
        place += len(PLACES[b])
    return ended(b, place - back)


class Count:

    def __init__(self, eng, sem):
        self.eng, self.sem, self.n, self.base = eng, sem, 0, 0
        self.last = sem, 0

    def mark(self, ins):
        self.n += 1
        self.last = self.sem, self.base + self.n
        return ins.then_inc(self.sem, 1)

    def tell(self, ins, sem, value):
        self.last = sem, value
        return ins.then_inc(sem, 1)

    def sync(self):
        wait(self.eng, *self.last)


def tiles(eng, count, n, body):
    c0 = count.n if count else 0
    body(0)
    if count:
        per = count.n - c0
    with eng.Fori(1, n) as i:
        if count:
            count.base = (i - 1) * per
        body(i)
    if count:
        count.base = 0
        count.n = c0 + n * per


def bc(ap, axis, n):
    a = ap.unsqueeze(axis)
    shape = list(a.shape)
    shape[axis] = n
    return a.broadcast_to(shape)


def encoder(nc, I, O):
    ctx = ExitStack()
    with ctx:
        sem_made = {}

        def sem(name):
            if name not in sem_made:
                sem_made[name] = ctx.enter_context(nc.semaphore(name))
            return sem_made[name]

        ARENA = 53000
        mem = ctx.enter_context(nc.sbuf_tensor("mem", [P, ARENA], F32))
        psum = ctx.enter_context(nc.psum_tensor("psum", [P, 8, 512], F32))
        at = [0]

        def take(*shape):
            n = int(np.prod(shape))
            ap = mem[:, at[0]:at[0] + n]
            at[0] += n
            assert at[0] <= ARENA, at[0]
            if len(shape) > 1:
                names = "abcd"[:len(shape)]
                ap = ap.rearrange(f"p ({' '.join(names)}) -> p {' '.join(names)}",
                                  **{k: s for k, s in zip(names[1:], shape[1:])})
            return ap

        HT = take(KT, TOK)
        YT = take(KT, TOK)
        ident = take(P)
        gate = take(2, D)
        modT = take(16, 9)
        npre = take(2, KT)
        cT, scT, ctmp = take(KT, 9), take(KT, 9), take(KT, 9)
        stat = take(16)
        halfneg = take(8)
        fixed_end = at[0]
        X = take(NT, D)
        x_end = at[0]

        def tok(ap, t):
            return ap[:, :, bass.ds(t * P, P)]

        mw = take(2, 3 * D)
        modb, modrow, npost = take(3 * D), take(3 * D), take(D)
        sel = take(2, P)
        mod_end = at[0]
        nj, xh = take(D), take(D)
        at[0] = x_end
        wqkv = take(KT, 768)
        ring_at = at[0]
        w0 = take(2, KT, P)
        UA = take(LM, UW)
        th = take(2, NC)
        cw0 = take(LM, TAPS + 1)
        gbias = take(LM, 2)
        lam, ksp, ksp2, kneg = take(LM), take(LM), take(LM), take(LM)
        ltmp = take(4, LM)
        h0, hc = take(LM, NS), take(LM, 1 + NS)
        cb0 = take(LM, 1 + NS, PRE)
        gw = take(2, P)
        cv_row = take(UW)
        cv = cv_row[:, 0:UC]
        xc, tr, ti, la, lw_, lg = (take(TOK) for _ in range(6))
        lh = cv_row[:, 0:TOK]
        lru_end = at[0]
        at[0] = ring_at
        hst = take(KT, P)
        amask = take(2, 2 * WIN)
        smask = take(NS, 2 * WIN)
        rope = take(NT, 32)
        QK, ra, rb = take(10, HD), take(10, 16), take(10, 16)
        SS = take(8, 2 * WIN)
        PT = take(2, 4, P)
        qT = take(4, P)
        kT, V = take((NT + 1) * P), take(NT + 1, P)
        kc, vc = take(NS, P), take(NS, P)
        kw, vw = take(2 * P), take(2, P)
        mx, m2, nm, es, den, d2, rd = (take(8) for _ in range(7))
        sinkP, sinkS = take(8), take(1)
        att_end = at[0]
        at[0] = x_end
        wout = take(KT, D)
        yst, oj, otmp = take(KT, P), take(D), take(D)
        assert at[0] <= ARENA
        at[0] = fixed_end
        wr = take(4, KT, P)
        U1 = take(3, UW)
        CV = take(3, UW)
        TH1 = take(UW)
        zt = take(2, NC)
        S1 = take(3, TOK)
        rowb = take(2, TOK)
        KN, KNT, KD, VB = take(4, P), take(4, P), take(4, P), take(4, P)
        EA, EQ, UM, LV = take(4, P), take(4, P), take(4, P), take(2, 4, P)
        XI, YI, WI, OO, ON = take(4, P), take(4, P), take(4, P), take(4, P), take(4, P)
        SQJ = take(P)
        RR, VN, QE, SP = take(P), take(P), take(P), take(P)
        SS1 = take(NS, P)
        VM = take(NS, P)
        KQ = take(2, P)
        KQS = take(2, P)
        HC = take(5, NT)
        CA = take(5, NT, H)
        EG = take(H, 16)
        MU = take(2, 2, P)
        LM1 = take(7, P)
        M8 = take(NS)
        CW = take(3 * H, TAPS)
        HN = take(1)
        CB1 = take(3 * H, 1 + NS, PRE)
        ssk, ssq, sso, rk, f1, f2, fo = (take(4) for _ in range(7))
        wba = mem[:, 0:0]
        l1_end = at[0]
        at[0] = fixed_end + 4 * KT * P
        wba = take(KT, 40)
        Z, Z1, Z2, GR = take(2, TOK), take(2, TOK), take(2, TOK), take(3, TOK)
        reset = take(TOK)
        nega, dtb, GL = take(1), take(1), take(16)
        assert at[0] <= ARENA
        at[0] = fixed_end
        wout1 = take(KT, D)
        XT = take(2, D)
        yst1, oj1, otmp1 = take(KT, P), take(D), take(D)
        x1_dram = nc.dram_tensor("x1_dram", (P, NT, D), F32, kind="Internal").ap()
        row_dram = nc.dram_tensor("row_dram", (H, 2, TOK), F32, kind="Internal").ap()
        eg_dram = nc.dram_tensor("eg_dram", (H, 16), F32, kind="Internal").ap()


        block = ctx.enter_context(nc.Block())
        B = lambda b: psum[:, b, :]

        def knt(b, i):
            return KNT[:, i] if b < 2 else KQ[:, 0]


        @block.sync
        def _(sp):
            PASSED[sp.engine] = sem("sp_passed")
            for ap, name in ((ident, "ident"), (cT, "cT"), (npre, "npre")):
                sp.dma_start(ap, I[name]).then_inc(sem("const_in"), 16)

            def mod_loads(l):
                sp.dma_start(sel[0:9], I["sel"]).then_inc(sem("modb_in"), 16)
                sp.dma_start(modb[0:9], I["modb"][l:l + 1, :].broadcast_to([9, 3 * D])
                             ).then_inc(sem("modb_in"), 16)
                sp.dma_start(npost[0:9], I["npost"][l:l + 1, :].broadcast_to([9, D])
                             ).then_inc(sem("modb_in"), 16)
                for k in range(KT):
                    if l or k >= 2:
                        sp.wait_ge(sem("mod_mm"), k - 1 + l * KT)
                    sp.dma_start(mw[:, k % 2], I["modw"][l, k]).then_inc(sem(f"mw_in{k % 2}"), 16)

            sp.dma_start(X, I["x"]).then_inc(sem("x_in"), 16)
            mod_loads(0)
            sp.wait_ge(sem("mod_tr"), 1)
            sp.wait_ge(sem("n_tp"), NT)
            sp.dma_start(wqkv, I["wqkv"]).then_inc(sem("wqkv_in"), 16)
            for ap, name in ((cw0, "cw0"), (gbias, "gbias"), (lam, "lam"), (h0, "h0")):
                sp.dma_start(ap, I[name]).then_inc(sem("lru_in"), 16)
            for m in range(LM):
                sp.dma_start(UA[:, m, US:].rearrange("p (s u) -> p s u", s=NS)[:, :, 0:PRE],
                             I["cs0"][:, m]).then_inc(sem("lru_in"), 16)
            for c in range(4):
                if c >= 2:
                    sp.wait_ge(sem("xa_mm"), 3 * (c - 1))
                sp.dma_start(w0[:, c % 2], I["w0"][c]).then_inc(sem(f"w0_in{c % 2}"), 16)

            def gate_loads(m):
                for q in range(2):
                    if isinstance(m, int) and m == 0:
                        sp.wait_ge(sem("xa_mm"), 3 * (3 + q))
                    else:
                        sp.wait_ge(sem("g_mm"), 6 * m + 3 * q - 3)
                    sp.dma_start(w0[:, q], I["w0"][bass.ds(m * 2 + (4 + q), 1)]
                                 .rearrange("a p k c -> p (a k) c")).then_inc(sem(f"w0_in{q}"), 16)
                if not (isinstance(m, int) and m == 0):
                    sp.wait_ge(sem("l_mm"), 6 * m)
                sp.dma_start(gw, I["gw"][bass.ds(m, 1)].rearrange("a p k c -> p (a k) c")
                             ).then_inc(sem("gw_in"), 16)

            tiles(sp, None, LM, gate_loads)
            sp.wait_ge(sem("l_y"), LM)
            sp.wait_ge(sem("hist0"), 2 * LM)
            sp.dma_start(O["cb0"], cb0).then_inc(sem("out0"), 16)
            sp.dma_start(O["hc"], hc).then_inc(sem("out0"), 16)
            sp.wait_ge(sem("out0"), 32)
            sp.dma_start(amask, I["amask"]).then_inc(sem("att_in"), 16)
            sp.dma_start(smask.rearrange("p s k -> p (s k)"),
                         I["smask"].broadcast_to([P, NS * 2 * WIN])).then_inc(sem("att_in"), 16)
            sp.dma_start(rope, I["rope"]).then_inc(sem("att_in"), 16)
            sp.dma_start(kc, I["kc"]).then_inc(sem("att_in"), 16)
            sp.dma_start(vc, I["vc"]).then_inc(sem("att_in"), 16)
            sp.dma_start(sinkP, I["sinkP"].broadcast_to([P, 8])).then_inc(sem("att_in"), 16)
            sp.dma_start(sinkS, I["sinkS"]).then_inc(sem("att_in"), 16)
            for q, t in enumerate((7, 8)):
                sp.wait_ge(sem("rope_done"), t + 1)
                sp.dma_start(O["kout"][q], QK[:, 8:10]).then_inc(sem("kout"), 16)
            for q, t in enumerate((7, 8)):
                sp.dma_start(O["vout"][q], V[:, t + 1]).then_inc(sem("out0"), 16)
            sp.wait_ge(sem("o_ev"), NT)
            sp.wait_ge(sem("out0"), 64)
            sp.wait_ge(sem("kout"), 32)
            sp.dma_start(wout, I["wout"][0]).then_inc(sem("wout_in"), 16)
            sp.wait_ge(sem("x1_done"), NT)
            sp.dma_start(x1_dram, X).then_inc(sem("x1_out"), 16)
            mod_loads(1)
            sp.wait_ge(sem("n_tp"), 2 * NT)
            sp.wait_ge(sem("x1_out"), 16)
            for ap, name in ((wba, "wba"), (reset[0:H], "reset"), (nega[0:H], "alog"), (dtb[0:H], "dtb")):
                sp.dma_start(ap, I[name]).then_inc(sem("ba_in"), 16)
            sp.wait_ge(sem("rows_ready"), 1)
            sp.dma_start(row_dram[:, 0], GR[0:H, 0]).then_inc(sem("rows_out"), 16)
            sp.dma_start(row_dram[:, 1], GR[0:H, 1]).then_inc(sem("rows_out"), 16)
            sp.dma_start(eg_dram, GL[0:H]).then_inc(sem("rows_out"), 16)
            sp.wait_ge(sem("rows_out"), 48)
            sp.wait_ge(sem("col_tr"), 1)
            for ap, name in ((MU, "maskU"), (LM1, "lmask"), (M8, "mask8"), (CW, "cw1"), (HN, "hn")):
                sp.dma_start(ap, I[name]).then_inc(sem("l1_in"), 16)
            sp.dma_start(EG.rearrange("p h g -> p (h g)"),
                         eg_dram.rearrange("(a h) g -> a (h g)", a=1).broadcast_to([P, H * 16])
                         ).then_inc(sem("l1_in"), 16)
            for m in range(3):
                sp.dma_start(U1[:, m, US:].rearrange("p (s u) -> p s u", s=NS)[:, :, 0:PRE],
                             I["cs1"][:, m]).then_inc(sem("cs_in"), 16)

            def weights(h, m):
                sp.dma_start(wr[:, m], I["w1"][bass.ds(h * 4 + m, 1)]
                             .rearrange("a p k c -> p (a k) c")).then_inc(sem(f"w1_in{m}"), 16)

            def rows(h):
                sp.dma_start(rowb.rearrange("p a t -> p (a t)"),
                             row_dram[bass.ds(h, 1)].rearrange("a q t -> a (q t)")
                             .broadcast_to([P, 2 * TOK])).then_inc(sem("rowb_in"), 16)

            for m in range(4):
                weights(0, m)
            rows(0)
            for m in range(4):
                sp.wait_ge(sem("pj_mm"), 3 * m + 3)
                weights(1, m)

            def head(h, ahead):
                if ahead:
                    wait(sp, sem("cv_done"), 3 * h + 3)
                    wait(sp, sem("hist1"), 6 * h + 6)
                    for m in range(3):
                        sp.dma_start(U1[:, m, US:].rearrange("p (s u) -> p s u", s=NS)[:, :, 0:PRE],
                                     I["cs1"][:, bass.ds((h + 1) * 3 + m, 1)]
                                     .rearrange("p a s u -> p (a s) u")).then_inc(sem("cs_in"), 16)
                if not (isinstance(h, int) and h == 0):
                    sp.wait_ge(sem("ss_out"), 16 * h)
                sp.dma_start(SS1, I["gs"][bass.ds(h, 1)].rearrange("a p s v -> p (a s) v")
                             ).then_inc(sem("ss_in"), 16)
                if ahead > 1:
                    for m in range(3):
                        sp.wait_ge(sem("pj_mm"), 12 * h + 3 * m + 15)
                        weights(h + 2, m)
                sp.wait_ge(sem("st_ready"), 9 * h + 9)
                sp.dma_start(O["sp"][bass.ds(h, 1)].rearrange("a p v -> p (a v)"), SP
                             ).then_inc(sem("sp_out"), 16)
                if ahead:
                    sp.wait_ge(sem("e_arg"), 3 * h + 3)
                    rows(h + 1)
                if ahead > 1:
                    sp.wait_ge(sem("pj_mm"), 12 * h + 24)
                    weights(h + 2, 3)
                sp.wait_ge(sem("ss_ready"), h + 1)
                sp.dma_start(O["ss"][bass.ds(h, 1)].rearrange("a p s v -> p (a s) v"), SS1
                             ).then_inc(sem("ss_out"), 16)

            tiles(sp, None, H - 2, lambda h: head(h, 2))
            head(H - 2, 1)
            head(H - 1, 0)
            sp.wait_ge(sem("hist1"), 6 * H)
            sp.dma_start(O["cb1"], CB1).then_inc(sem("out1"), 16)
            sp.wait_ge(sem("y1_done"), 3 * H)
            sp.wait_ge(sem("sp_out"), 16 * H)
            sp.wait_ge(sem("ss_out"), 16 * H)
            sp.wait_ge(sem("out1"), 16)
            sp.dma_start(wout1, I["wout"][1]).then_inc(sem("wout1_in"), 16)

            def last(t):
                first = isinstance(t, int) and t == 0
                if not first:
                    sp.wait_ge(sem("y_out"), 16 * t)
                sp.dma_start(XT[:, 0], x1_dram[:, bass.ds(t, 1)].rearrange("p a d -> p (a d)")
                             ).then_inc(sem("xt_in"), 16)
                sp.wait_ge(sem("x1_done"), NT + t + 1)
                sp.dma_start(O["y"][:, bass.ds(t, 1)].rearrange("p a d -> p (a d)"), XT[:, 0]
                             ).then_inc(sem("y_out"), 16)

            tiles(sp, None, NT, last)
            sp.wait_ge(sem("y_out"), 16 * NT)

        @block.gpsimd
        def _(pool):
            c = Count(pool, sem("pool_own"))
            PASSED[pool.engine] = sem("pool_passed")
            c.mark(pool.memset(halfneg, -0.5))
            c.sync()

            def norm(T):
                wait(pool, sem("n_ss"), T + 1)
                c.mark(pool.tensor_scalar(stat[:, 1:2], stat[:, 0:1], 1.0 / D, EPS, ALU.mult, ALU.add))
                c.sync()
                pool.tensor_tensor(stat[:, 2:3], stat[:, 1:2], halfneg[:, 0:1], ALU.pow
                                   ).then_inc(sem("n_rs"), 1)

            tiles(pool, c, NT, norm)
            wait(pool, sem("n_tp"), NT)
            pool.memset(UA[:, :, 0:PRE], 0.0).then_inc(sem("ua_zero"), 1)

            def hist(m):
                if isinstance(m, int):
                    wait(pool, sem("xa_ev"), 12)
                    wait(pool, sem("lru_in"), 16 * 8)
                pool.tensor_copy(cb0[:, bass.ds(m, 1), 0], UA[:, bass.ds(m, 1), SEQ:SEQ + PRE]
                                 ).then_inc(sem("hist0"), 1)
                s = UA[:, m, US:].rearrange("p (s u) -> p s u", s=NS)[:, :, DS:]
                pool.tensor_copy(cb0[:, m, 1:], s).then_inc(sem("hist0"), 1)

            for m in range(LM):
                hist(m)
            c.sync()
            wait(pool, sem("l_y"), LM)
            wait(pool, sem("out0"), 32)
            c.mark(pool.memset(kT[:, 0:P], 0.0))
            c.mark(pool.memset(V[:, 0], 0.0))

            def stage(t):
                if not (isinstance(t, int) and t == 0):
                    wait(pool, sem("qkv_mm"), t)
                pool.tensor_copy(hst, tok(HT, t)).then_inc(sem("hst_ready"), 1)

            def window(t):
                wait(pool, sem("qT_ev"), t + 1)
                if not (isinstance(t, int) and t == 0):
                    wait(pool, sem("s_mm"), 4 * t)
                pool.tensor_copy(kw, kT[:, bass.ds(t * P, 2 * P)]).then_inc(sem("kw_ready"), 1)
                stage(t + 1)
                if not (isinstance(t, int) and t == 0):
                    wait(pool, sem("pv_mm"), 4 * t)
                pool.tensor_copy(vw, V[:, bass.ds(t, 2)]).then_inc(sem("vw_ready"), 1)

            c.sync()
            stage(0)
            tiles(pool, None, NT - 1, window)

            def out(T, t, win, stage_to):
                if isinstance(T, int) and T in (0, NT):
                    wait(pool, sem(win), 16)
                if not (isinstance(T, int) and T == 0):
                    wait(pool, sem("out_mm"), T)
                pool.tensor_copy(stage_to, tok(YT, t)).then_inc(sem("yst_ready"), 1)
                wait(pool, sem("o_ss"), T + 1)
                c.mark(pool.tensor_tensor(stat[:, 6:7], stat[:, 4:5], stat[:, 5:6], ALU.add))
                c.sync()
                c.mark(pool.tensor_scalar(stat[:, 7:8], stat[:, 6:7], 1.0 / D, EPS, ALU.mult, ALU.add))
                c.sync()
                pool.tensor_tensor(stat[:, 8:9], stat[:, 7:8], halfneg[:, 0:1], ALU.pow
                                   ).then_inc(sem("o_rs"), 1)

            tiles(pool, c, NT, lambda t: out(t, t, "wout_in", yst))
            tiles(pool, c, NT, lambda t: norm(t + NT))
            wait(pool, sem("l1_in"), 16 * 6)
            wait(pool, sem("rows_out"), 48)
            wait(pool, sem("col_tr"), 1)
            pool.memset(U1[:, :, 0:PRE], 0.0).then_inc(sem("u1_zero"), 1)

            def hist1(h):
                wait(pool, sem("pj_ev"), 9 * h + 9)
                wait(pool, sem("cs_in"), 48 * h + 48)
                for m in range(3):
                    pool.tensor_copy(CB1[:, bass.ds(h * 3 + m, 1), 0], U1[:, m:m + 1, SEQ:US]
                                     ).then_inc(sem("hist1"), 1)
                    pool.tensor_copy(
                        CB1[:, bass.ds(h * 3 + m, 1), 1:].rearrange("p a s u -> p (a s) u"),
                        U1[:, m, US:].rearrange("p (s u) -> p s u", s=NS)[:, :, DS:]
                    ).then_inc(sem("hist1"), 1)

            def delta(h, b):
                nb = 4 if b < 2 else 1
                T = 3 * h + b
                wait(pool, sem("ssk"), T + 1)
                c.mark(pool.tensor_scalar(rk[:, 0:nb], ssk[:, 0:nb], 4 * EPS, None, ALU.add))
                c.sync()
                c.tell(pool.tensor_tensor(rk[:, 0:nb], rk[:, 0:nb], halfneg[:, 0:nb], ALU.pow),
                       sem("rk_ready"), T + 1)
                wait(pool, sem("kn_ready"), T + 1)
                pool.tensor_tensor(KD[:, 0:nb], KN[:, 0:nb], bc(HC[:, 4, 4 * b:4 * b + nb], 2, P),
                                   ALU.mult).then_inc(sem("kd_ready"), 1)
                if b == 2:
                    wait(pool, sem("s1_ready"), 3 * h + 3)
                    pool.tensor_copy(KQ[:, 1], S1[:, 0, SEQ:]).then_inc(sem("kq_ready"), 1)
                wait(pool, sem("um_ready"), T + 1)
                for lv in range(7 if b < 2 else 4):
                    L0 = 18 * h + 7 * b
                    if lv >= 2:
                        if lv == 2:
                            wait(pool, sem("y0_ready"), T + 1)
                        else:
                            wait(pool, sem("w_mm"), 15 * h + 6 * b + lv - 2)
                    pool.tensor_tensor(LV[:, lv % 2, 0:nb], UM[:, 0:nb], bc(LM1[:, lv], 1, nb),
                                       ALU.mult).then_inc(sem("lv_ready"), 1)
                wait(pool, sem("ssq"), T + 1)
                c.mark(pool.tensor_scalar(f1[:, 0:nb], ssq[:, 0:nb], P * EPS, 4 * P * EPS * EPS,
                                          ALU.mult, ALU.add))
                wait(pool, sem("sso"), T + 1)
                c.mark(pool.tensor_scalar(f2[:, 0:nb], sso[:, 0:nb], 1.0 / P, None, ALU.mult))
                c.sync()
                c.mark(pool.tensor_tensor(f2[:, 0:nb], f2[:, 0:nb], f1[:, 0:nb], ALU.add))
                c.sync()
                c.tell(pool.tensor_tensor(fo[:, 0:nb], f2[:, 0:nb], halfneg[:, 0:nb], ALU.pow),
                       sem("fo_ready"), T + 1)

            def head(h, ahead=True):
                for b in range(3):
                    delta(h, b)
                if ahead:
                    hist1(h + 1)

            hist1(0)
            tiles(pool, c, H - 1, head)
            head(H - 1, False)
            wait(pool, sem("wout1_in"), 16)
            tiles(pool, c, NT, lambda t: out(t + NT, t, "wout1_in", yst1))

        @block.tensor
        def _(pe):
            def mm(*a, **k):
                return pe.matmul(*a, **k)

            def tr(out, in_, n=P):
                return pe.transpose(out, in_, ident[0:n, 0:n])

            def mod(l):
                pe.wait_ge(sem("sc_ready"), 1)
                pe.wait_ge(sem("const_in"), 48)
                for k in range(KT):
                    pe.wait_ge(sem(f"mw_in{k % 2}"), 16 * (k // 2 + 1) + 64 * l)
                    for n in range(6):
                        i = mm(B(n)[0:9], scT[:, k], mw[:, k % 2, n * 512:(n + 1) * 512],
                               start=(k == 0), stop=(k == KT - 1))
                    i.then_inc(sem("mod_mm"), 1)
                pe.wait_ge(sem("mod_row"), l + 1)
                for j in range(16):
                    tr(B(6)[:, 9 * j:9 * j + 9], modrow[0:9, j * P:(j + 1) * P], 9)
                for w in range(2):
                    for n in range(2):
                        i = mm(B(2 * w + n), sel[0:9, w],
                               modrow[0:9, 2 * D + n * 512:2 * D + (n + 1) * 512],
                               start=True, stop=True)
                i.then_inc(sem("mod_tr"), 1)

            def norm(T):
                pe.wait_ge(sem("n_xh"), T + 1)
                if isinstance(T, int) and T == 0:
                    pe.wait_ge(sem("mod_done"), 1)
                else:
                    pe.wait_ge(sem("n_ev"), T)
                for k in range(KT):
                    i = tr(B(6 + k // 4)[:, (k % 4) * P:(k % 4 + 1) * P], xh[:, k * P:(k + 1) * P])
                i.then_inc(sem("n_tp"), 1)

            mod(0)
            tiles(pe, None, NT, norm)
            pe.wait_ge(sem("n_ev"), NT)

            def project(c, slot, sname, wait):
                for n in range(3):
                    wait(n)
                    for k in range(KT):
                        i = mm(B(slot * 3 + n)[:, 0:NC], w0[:, slot, k], HT[:, k, n * NC:(n + 1) * NC],
                               start=(k == 0), stop=(k == KT - 1))
                    i.then_inc(sem(sname), 1)

            for c in range(4):
                pe.wait_ge(sem(f"w0_in{c % 2}"), 16 * (c // 2 + 1))
                project(c, c % 2, "xa_mm",
                        lambda n: pe.wait_ge(sem("xa_ev"), 3 * c + n - 5) if c >= 2 else None)

            def gates(m):
                first = isinstance(m, int) and m == 0
                for q in range(2):
                    pe.wait_ge(sem(f"w0_in{q}"), 16 * m + 48)
                    project(m, q, "g_mm",
                            lambda n: pe.wait_ge(sem("xa_ev"), 6 + 3 * q + n + 1) if first
                            else pe.wait_ge(sem("g_ev"), 6 * m + 3 * q + n - 5))
                pe.wait_ge(sem("gw_in"), 16 * m + 16)
                pe.wait_ge(sem("xc_ready"), m + 1)
                for i in range(6):
                    if not first or i >= 2:
                        pe.wait_ge(sem("lz_ev"), 6 * m + i - 1)
                    mm(B(6 + i % 2)[:, 0:NC], gw[:, i // 3], xc[:, (i % 3) * NC:(i % 3 + 1) * NC],
                       start=True, stop=True).then_inc(sem("l_mm"), 1)

            tiles(pe, None, LM, gates)
            pe.wait_ge(sem("g_ev"), 6 * LM)
            pe.wait_ge(sem("lz_ev"), 6 * LM)
            pe.wait_ge(sem("wqkv_in"), 16)
            pe.wait_ge(sem("att_in"), 16 * 7)

            def qkv(t):
                pe.wait_ge(sem("hst_ready"), t + 1)
                if not (isinstance(t, int) and t == 0):
                    pe.wait_ge(sem("qkv_ev"), t)
                for b, lo, n in ((0, 0, 512), (1, 512, 256)):
                    for k in range(KT):
                        i = mm(B(b)[:, 0:n], hst[:, k], wqkv[:, k, lo:lo + n],
                               start=(k == 0), stop=(k == KT - 1))
                i.then_inc(sem("qkv_mm"), 1)

            def att(t):
                first = isinstance(t, int) and t == 0
                sample = isinstance(t, int) and t == NT - 1
                pe.wait_ge(sem("rope_done"), t + 1)
                if not first:
                    pe.wait_ge(sem("qT_ev"), t)
                    pe.wait_ge(sem("o_ev"), t)
                for j in range(4):
                    tr(B(2)[:, j * P:(j + 1) * P], QK[:, 2 * j:2 * j + 2].rearrange("p v d -> p (v d)"))
                tr(B(3)[:, 0:P], QK[:, 8:10].rearrange("p v d -> p (v d)")).then_inc(sem("qk_tp"), 1)
                pe.wait_ge(sem("qT_ev"), t + 1)
                if not sample:
                    pe.wait_ge(sem("kw_ready"), t + 1)
                for u in range(4):
                    if not first or u >= 2:
                        pe.wait_ge(sem("s_add"), 4 * t + u - 1)
                    for a in range(2):
                        if sample:
                            s = 2 * u + a
                            for v in range(2):
                                vs = slice(v * HD, (v + 1) * HD)
                                q = qT.rearrange("p j t -> p (j t)")[vs, s * 64:(s + 1) * 64]
                                mm(B(4 + u % 2)[vs, a * 256:a * 256 + P], q, kc[vs, s],
                                   start=True, stop=True)
                                i = mm(B(4 + u % 2)[vs, a * 256 + P:a * 256 + 256], q,
                                       kT[vs, NT * P:(NT + 1) * P], start=True, stop=True)
                        else:
                            v, j = u // 2, 2 * (u % 2) + a
                            vs = slice(v * HD, (v + 1) * HD)
                            i = mm(B(4 + u % 2)[:, a * 256:(a + 1) * 256], qT[vs, j],
                                   kw[vs], start=True, stop=True)
                    i.then_inc(sem("s_mm"), 1)
                if not sample:
                    qkv(t + 1)
                    pe.wait_ge(sem("vw_ready"), t + 1)
                for u in range(4):
                    pe.wait_ge(sem("p_norm"), 4 * t + u + 1)
                    if not first or u >= 2:
                        pe.wait_ge(sem("pt_ev"), 4 * t + u - 1)
                    for a in range(2):
                        for w in range(2):
                            i = tr(B(6 + u % 2)[:, (2 * a + w) * P:(2 * a + w + 1) * P],
                                   SS[:, 2 * u + a, w * P:(w + 1) * P])
                    i.then_inc(sem("pt_tp"), 1)
                    pe.wait_ge(sem("pt_ev"), 4 * t + u + 1)
                    for a in range(2):
                        if sample:
                            s = 2 * u + a
                            for v in range(2):
                                vs = slice(v * HD, (v + 1) * HD)
                                o = B(3)[vs, s * HD:(s + 1) * HD]
                                mm(o, vc[:, s, vs], PT[:, u % 2, 2 * a, vs], start=True, stop=False)
                                i = mm(o, V[:, NT, vs], PT[:, u % 2, 2 * a + 1, vs],
                                       start=False, stop=True)
                        else:
                            v, j = u // 2, 2 * (u % 2) + a
                            o = B(3)[v * HD:(v + 1) * HD, j * P:(j + 1) * P]
                            for w in range(2):
                                i = mm(o, vw[:, w, v * HD:(v + 1) * HD], PT[:, u % 2, 2 * a + w],
                                       start=(w == 0), stop=(w == 1))
                    i.then_inc(sem("pv_mm"), 1)

            qkv(0)
            tiles(pe, None, 7, att)
            att(7)
            att(8)
            pe.wait_ge(sem("o_ev"), NT)
            pe.wait_ge(sem("wout_in"), 16)

            def out(T, st, w):
                pe.wait_ge(sem("yst_ready"), T + 1)
                if not (isinstance(T, int) and T == 0):
                    pe.wait_ge(sem("out_ev"), T)
                for n in range(2):
                    for k in range(KT):
                        i = mm(B(n), st[:, k], w[:, k, n * 512:(n + 1) * 512],
                               start=(k == 0), stop=(k == KT - 1))
                i.then_inc(sem("out_mm"), 1)

            tiles(pe, None, NT, lambda t: out(t, yst, wout))
            pe.wait_ge(sem("out_ev"), NT)
            mod(1)
            pe.wait_ge(sem("mod_done"), 2)
            tiles(pe, None, NT, lambda t: norm(t + NT))
            pe.wait_ge(sem("n_ev"), 2 * NT)

            pe.wait_ge(sem("ba_in"), 64)
            for n in range(3):
                for k in range(KT):
                    i = mm(B(n)[0:40, 0:NC], wba[:, k], HT[:, k, n * NC:(n + 1) * NC],
                           start=(k == 0), stop=(k == KT - 1))
            i.then_inc(sem("ba_mm"), 1)
            pe.wait_ge(sem("rows_ready"), 1)
            for q in range(3):
                for t in range(NT):
                    i = tr(B(3)[:, (q * NT + t) * H:(q * NT + t + 1) * H],
                           GR[0:H, q, t * P:(t + 1) * P], H)
            i.then_inc(sem("col_tr"), 1)

            def product(h, j):
                g, k = divmod(j, KT)
                m, n = divmod(g, 3)
                if k == 0:
                    if n == 0:
                        pe.wait_ge(sem(f"w1_in{m}"), 16 * h + 16)
                    if g < 2:
                        if not (isinstance(h, int) and h == 0):
                            pe.wait_ge(sem("z_ev"), 3 * h + g - 1)
                    elif g < 11:
                        pe.wait_ge(sem("pj_ev"), 9 * h + g - 1)
                    else:
                        pe.wait_ge(sem("z_ev"), 3 * h + 1)
                i = mm(B(g % 2)[:, 0:NC], wr[:, m, k], HT[:, k, n * NC:(n + 1) * NC],
                       start=(k == 0), stop=(k == KT - 1))
                if k == KT - 1:
                    i.then_inc(sem("pj_mm"), 1)

            def delta(h, b, ahead):
                first = isinstance(h, int) and h == 0 and b == 0
                nb = 4 if b < 2 else 1
                T = 3 * h + b
                col = lambda m, i: S1[:, m, (4 * b + i) * P:(4 * b + i + 1) * P]
                at_ = lambda bk, i: B(bk)[:, i * P:(i + 1) * P]
                place = iter(range(len(PLACES[b])))

                def between():
                    for j in range(*PLACES[b][next(place)]):
                        if ahead:
                            product(h + 1, j)

                pe.wait_ge(sem("s1_ready"), 3 * h + 3)
                if not first:
                    pe.wait_ge(sem("y1_done"), T)
                for m, bk, name in ((1, 2, "tk"), (0, 3, "tq"), (2, 4, "tv")):
                    for i in range(nb):
                        x = tr(at_(bk, i), col(m, i))
                    x.then_inc(sem(name), 1)
                between()
                pe.wait_ge(sem("kn_ready"), T + 1)
                for i in range(nb):
                    x = tr(at_(5, i), KN[:, i])
                x.then_inc(sem("tkn"), 1)
                between()
                pe.wait_ge(sem("knt_ready"), T + 1)
                pe.wait_ge(sem("ssq"), T + 1)
                for i in range(nb):
                    mm(at_(2, i), knt(b, i), knt(b, i), start=True, stop=True)
                    x = mm(at_(3, i), knt(b, i), col(0, i), start=True, stop=True)
                x.then_inc(sem("gq_mm"), 1)
                W0, L0, X0 = 15 * h + 6 * b, 18 * h + 7 * b, 16 * h + 6 * b
                between()
                pe.wait_ge(sem("vb_ready"), T + 1)
                pe.wait_ge(sem("y0_ready"), T + 1)
                for i in range(nb):
                    x = tr(at_(4, i), YI[:, i])
                x.then_inc(sem("x_tp"), 1)
                levels = 6 if b < 2 else 3
                for lv in range(1, levels + 1):
                    pe.wait_ge(sem("lv_ready"), L0 + lv + 1)
                    pe.wait_ge(sem("xi_ready" if lv == 1 else "n_ev1"), T + 1 if lv == 1 else W0 + lv - 1)
                    for i in range(nb):
                        x = mm(at_(5, i), LV[:, lv % 2, i], XI[:, i], start=True, stop=True)
                    x.then_inc(sem("w_mm"), 1)
                    between()
                    pe.wait_ge(sem("w_ev"), W0 + lv)
                    if lv > 1:
                        pe.wait_ge(sem("y_ev"), 13 * h + 5 * b + lv - 1)
                    for i in range(nb):
                        if lv < 6:
                            x = mm(at_(2, i), YI[:, i], WI[:, i], start=True, stop=True)
                        else:
                            x = mm(at_(2, i), WI[:, i], YI[:, i], start=True, stop=True)
                    x.then_inc(sem("n_mm"), 1)
                    between()
                    pe.wait_ge(sem("n_ev1"), W0 + lv)
                    if lv < 6:
                        for i in range(nb):
                            x = tr(at_(4, i), XI[:, i])
                        x.then_inc(sem("x_tp"), 1)
                        between()
                if b == 2:
                    pe.wait_ge(sem("y_ev"), 13 * h + 13)
                pe.wait_ge(sem("kd_ready"), T + 1)
                pe.wait_ge(sem("qkt_ready"), T + 1)
                for i in range(nb):
                    c = 9 * h + 4 * b + i
                    if b < 2:
                        pe.wait_ge(sem("st_ready"), c + 1)
                        mm(at_(6, 0), knt(b, i), SP, start=True, stop=True).then_inc(sem("ks_mm"), 1)
                        if not (first and i == 0):
                            pe.wait_ge(sem("o_ready"), c)
                        mm(at_(7, 0), col(0, i), SP, start=True, stop=True).then_inc(sem("qs_mm"), 1)
                    else:
                        pe.wait_ge(sem("ss_in"), 16 * h + 16)
                        pe.wait_ge(sem("kq_ready"), h + 1)
                        pe.wait_ge(sem("st_ready"), c + 1)
                        pe.wait_ge(sem("o_ready"), c)
                        for s_ in range(NS):
                            x = mm(B(6)[:, s_ * 32:(s_ + 1) * 32], SS1[:, s_],
                                   KQ[:, :, s_ * DS:(s_ + 1) * DS], start=True, stop=True)
                        x.then_inc(sem("kqs_mm"), 1)
                        between()
                        pe.wait_ge(sem("kqs_ev"), h + 1)
                        tr(at_(6, 0), KQS[:, 0]).then_inc(sem("ks_mm"), 1)
                        tr(at_(7, 0), KQS[:, 1]).then_inc(sem("qs_mm"), 1)
                    between()
                    pe.wait_ge(sem("r_ready"), c + 1)
                    mm(at_(6, 1), YI[:, i], RR, start=True, stop=True).then_inc(sem("tr_mm"), 1)
                    between()
                    pe.wait_ge(sem("vn_ready"), c + 1)
                    if b < 2:
                        mm(at_(6, 2), KD[:, i], VN, start=True, stop=True).then_inc(sem("kv_mm"), 1)
                    pe.wait_ge(sem("qe_ready"), c + 1)
                    mm(at_(7, 1), EQ[:, i], VN, start=True, stop=True).then_inc(sem("o_mm"), 1)
                    if b == 2:
                        pe.wait_ge(sem("vm_ready"), h + 1)
                        for g in range(2):
                            x = mm(B(4 + g), KD[:, 0], VM[:, 4 * g:4 * g + 4].rearrange("p s v -> p (s v)"),
                                   start=True, stop=True)
                        x.then_inc(sem("skv_mm"), 1)
                    between()
                between()
                pe.wait_ge(sem("on_ready"), T + 1)
                for i in range(nb):
                    x = tr(at_(2, i), ON[:, i])
                x.then_inc(sem("o_tp"), 1)
                between()
                assert not list(place)

            def head(h, ahead=True):
                for b in range(3):
                    delta(h, b, ahead)

            for j in range(GROUPS * KT):
                product(0, j)
            tiles(pe, None, H - 1, head)
            head(H - 1, False)
            pe.wait_ge(sem("y1_done"), 3 * H)
            pe.wait_ge(sem("z_ev"), 3 * H)
            pe.wait_ge(sem("wout1_in"), 16)
            tiles(pe, None, NT, lambda t: out(t + NT, yst1, wout1))

        @block.scalar
        def _(act):
            c = Count(act, sem("act_own"))
            PASSED[act.engine] = sem("act_passed")
            wait(act, sem("const_in"), 48)
            act.activation(ctmp, cT, ACT.Tanh, scale=0.5).then_inc(sem("c_th"), 1)

            def norm(T, t):
                if isinstance(T, int) and T == 0:
                    wait(act, sem("x_in"), 16)
                act.activation(nj, X[:, bass.ds(t, 1)].rearrange("p a d -> p (a d)"), ACT.Square,
                               accum_out=stat[:, 0:1]).then_inc(sem("n_ss"), 1)
                wait(act, sem("n_rs"), T + 1)
                if not (isinstance(T, int) and T == 0):
                    wait(act, sem("n_tp"), T)
                act.activation(xh, X[:, bass.ds(t, 1)].rearrange("p a d -> p (a d)"), ACT.Copy,
                               scale=stat[:, 2:3]).then_inc(sem("n_xh"), 1)

            tiles(act, None, NT, lambda t: norm(t, t))
            wait(act, sem("lru_in"), 16 * 8)
            c.mark(act.activation(ltmp[:, 0], lam, ACT.Abs))
            c.sync()
            c.mark(act.activation(ltmp[:, 1], ltmp[:, 0], ACT.Exp, scale=-1.0))
            c.sync()
            act.activation(ltmp[:, 2], ltmp[:, 1], ACT.Ln, bias=1.0).then_inc(sem("sp_ln"), 1)
            for m in range(4):
                for n in range(3):
                    wait(act, sem("xa_mm"), 3 * m + n + 1)
                    b = B((m % 2) * 3 + n)
                    if n < 2:
                        i = act.activation(UA[:, m, PRE + n * NC:PRE + (n + 1) * NC], b[:, 0:NC], ACT.Copy)
                    else:
                        r = SEQ - 2 * NC
                        c.mark(act.activation(UA[:, m, PRE + 2 * NC:PRE + SEQ], b[:, 0:r], ACT.Copy))
                        i = act.activation(
                            UA[:, m, US:].rearrange("p (s u) -> p s u", s=NS)[:, :, PRE:],
                            b[:, r:NC].rearrange("p (s u) -> p s u", s=NS), ACT.Copy)
                    i.then_inc(sem("xa_ev"), 1)

            def lru(m):
                first = isinstance(m, int) and m == 0
                if first:
                    wait(act, sem("l_const"), 1)
                for g in range(6):
                    wait(act, sem("g_mm"), 6 * m + g + 1)
                    if not first or g >= 2:
                        wait(act, sem("g_ev"), 6 * m + g - 1)
                    act.activation(th[:, g % 2], B(g)[:, 0:NC], ACT.Tanh, scale=0.5
                                   ).then_inc(sem("g_th"), 1)
                for i in range(6):
                    wait(act, sem("l_mm"), 6 * m + i + 1)
                    if not first and i == 0:
                        wait(act, sem("l_y"), m)
                    dst = (tr, ti)[i // 3][:, (i % 3) * NC:(i % 3 + 1) * NC]
                    act.activation(dst, B(6 + i % 2)[:, 0:NC], ACT.Tanh, scale=0.5,
                                   bias=gbias[:, bass.ds(m, 1), i // 3]).then_inc(sem("lz_ev"), 1)
                wait(act, sem("lz_ev"), 6 * m + 3)
                c.mark(act.activation(la, tr, ACT.Exp, scale=ksp[:, bass.ds(m, 1)],
                                      bias=ksp[:, bass.ds(m, 1)]))
                act.activation(lw_, tr, ACT.Tanh, scale=kneg[:, bass.ds(m, 1)],
                               bias=kneg[:, bass.ds(m, 1)]).then_inc(sem("l_a"), 1)
                wait(act, sem("l_w"), m + 1)
                act.activation(lw_, lw_, ACT.Sqrt).then_inc(sem("l_sq"), 1)

            tiles(act, c, LM, lru)

            def qkv_ev(t):
                wait(act, sem("qkv_mm"), t + 1)
                if not (isinstance(t, int) and t == 0):
                    wait(act, sem("qk_tp"), t)
                if isinstance(t, int) and t == 0:
                    wait(act, sem("l_y"), LM)
                    wait(act, sem("out0"), 32)
                if isinstance(t, int) and t == 8:
                    wait(act, sem("kout"), 16)
                c.mark(act.activation(QK[:, 0:8].rearrange("p (j v) d -> p v j d", v=2),
                                      B(0).rearrange("p (v j d) -> p v j d", v=2, j=4), ACT.Copy))
                c.mark(act.activation(QK[:, 8:10].rearrange("p v d -> p (v d)"), B(1)[:, 0:P], ACT.Copy))
                act.activation(V[:, bass.ds(t + 1, 1)].rearrange("p a d -> p (a d)"), B(1)[:, P:2 * P],
                               ACT.Copy).then_inc(sem("qkv_ev"), 1)

            def att(t):
                first = isinstance(t, int) and t == 0
                wait(act, sem("qk_tp"), t + 1)
                if not first:
                    wait(act, sem("s_mm"), 4 * t)
                if isinstance(t, int) and t == NT - 1:
                    c.mark(act.activation(
                        qT.rearrange("p j t -> p (j t)").rearrange("p (s j u) -> p j s u", s=NS, j=4),
                        B(2).rearrange("p (j s u) -> p j s u", s=NS, j=4), ACT.Copy))
                else:
                    c.mark(act.activation(qT.rearrange("p j t -> p (j t)"), B(2), ACT.Copy))
                act.activation(kT[:, bass.ds(t * P + P, P)], B(3)[:, 0:P], ACT.Copy
                               ).then_inc(sem("qT_ev"), 1)
                wait(act, sem("s_stat"), t + 1)
                for a in range(8):
                    c.mark(act.activation(SS[:, a], SS[:, a], ACT.Exp, scale=HD ** -0.5,
                                          bias=nm[:, a:a + 1], accum_out=den[:, a:a + 1]))
                act.activation(es, es, ACT.Exp).then_inc(sem("p_exp"), 1)
                if not (isinstance(t, int) and t == 8):
                    qkv_ev(t + 1)
                for u in range(4):
                    wait(act, sem("pt_tp"), 4 * t + u + 1)
                    if not first or u >= 2:
                        wait(act, sem("pv_mm"), 4 * t + u - 1)
                    act.activation(PT[:, u % 2].rearrange("p a t -> p (a t)"), B(6 + u % 2), ACT.Copy
                                   ).then_inc(sem("pt_ev"), 1)

            qkv_ev(0)
            tiles(act, c, 7, att)
            att(7)
            att(8)

            def out(T, junk):
                for n in range(2):
                    if n == 0:
                        wait(act, sem("out_mm"), T + 1)
                    i = act.activation(junk[:, n * 512:(n + 1) * 512], B(n), ACT.Square,
                                       accum_out=stat[:, 4 + n:5 + n])
                    if n == 0:
                        c.mark(i)
                i.then_inc(sem("o_ss"), 1)

            tiles(act, c, NT, lambda t: out(t, oj))
            act.wait_ge(sem("x1_done"), NT)
            tiles(act, None, NT, lambda t: norm(t + NT, t))

            act.wait_ge(sem("ba_mm"), 1)
            act.wait_ge(sem("n_tp"), 2 * NT)
            for n in range(3):
                c.mark(act.activation(Z[0:H, 0, n * NC:(n + 1) * NC], B(n)[0:H, 0:NC], ACT.Copy, scale=-1.0))
                c.mark(act.activation(Z[0:H, 1, n * NC:(n + 1) * NC], B(n)[32:40, 0:NC], ACT.Copy))
            c.sync()
            c.mark(act.activation(Z[0:H, 1], Z[0:H, 1], ACT.Identity, bias=dtb[0:H]))
            c.sync()
            c.mark(act.activation(Z1[0:H], Z[0:H], ACT.Abs))
            c.sync()
            c.mark(act.activation(Z1[0:H], Z1[0:H], ACT.Exp, scale=-1.0))
            c.mark(act.activation(nega[0:H], nega[0:H], ACT.Exp))
            c.sync()
            act.activation(Z1[0:H], Z1[0:H], ACT.Ln, bias=1.0).then_inc(sem("ba_ln"), 1)
            act.wait_ge(sem("gl_ready"), 1)
            act.activation(GL[0:H], GL[0:H], ACT.Exp).then_inc(sem("rows_ready"), 1)
            act.wait_ge(sem("ca_arg"), 1)
            act.activation(CA[:, 1:], CA[:, 1:], ACT.Exp).then_inc(sem("ca_exp"), 1)
            act.wait_ge(sem("rows_out"), 48)

            def leave(h, g):
                first = isinstance(h, int) and h == 0
                m, n = divmod(g, 3)
                bk = B(g % 2)
                wait(act, sem("pj_mm"), 12 * h + g + 1)
                if m == 3:
                    if not first or n >= 2:
                        wait(act, sem("z_ev"), 3 * h + n - 1)
                    act.activation(zt[:, n % 2], bk[:, 0:NC], ACT.Tanh, scale=0.5
                                   ).then_inc(sem("z_th"), 1)
                    return
                if not first and n == 0:
                    wait(act, sem("cv_done"), 3 * h)
                    wait(act, sem("hist1"), 6 * h)
                if n < 2:
                    i = act.activation(U1[:, m, PRE + n * NC:PRE + (n + 1) * NC], bk[:, 0:NC], ACT.Copy)
                else:
                    r = SEQ - 2 * NC
                    c.mark(act.activation(U1[:, m, PRE + 2 * NC:US], bk[:, 0:r], ACT.Copy))
                    i = act.activation(
                        U1[:, m, US:].rearrange("p (s u) -> p s u", s=NS)[:, :, PRE:],
                        bk[:, r:NC].rearrange("p (s u) -> p s u", s=NS), ACT.Copy)
                i.then_inc(sem("pj_ev"), 1)

            def silu_tanh(h, m):
                wait(act, sem("cv_done"), 3 * h + m + 1)
                if not (isinstance(h, int) and h == 0 and m == 0):
                    wait(act, sem("s1_ready"), 3 * h + m)
                act.activation(TH1[:, 0:UC], CV[:, m, 0:UC], ACT.Tanh, scale=0.5
                               ).then_inc(sem("th1"), 1)

            def delta(h, b, ahead):
                nb = 4 if b < 2 else 1
                T = 3 * h + b
                W0 = 15 * h + 6 * b
                place = iter(range(len(PLACES[b])))

                def between():
                    p = next(place)
                    if ahead:
                        for g in ended(b, p):
                            leave(h + 1, g)
                        if b == 2 and p in (3, 6, 9):
                            silu_tanh(h + 1, p // 3 - 1)

                wait(act, sem("tk"), T + 1)
                for i in range(nb):
                    if i:
                        c.sync()
                    x = act.activation(SQJ, B(2)[:, i * P:(i + 1) * P], ACT.Square,
                                       accum_out=ssk[:, i:i + 1])
                    if i < nb - 1:
                        c.mark(x)
                c.tell(x, sem("ssk"), T + 1)
                wait(act, sem("e_arg"), T + 1)
                c.mark(act.activation(EA[:, 0:nb], EA[:, 0:nb], ACT.Exp))
                act.activation(EQ[:, 0:nb], EQ[:, 0:nb], ACT.Exp).then_inc(sem("e_exp"), 1)
                wait(act, sem("tq"), T + 1)
                wait(act, sem("ssk"), T + 1)
                for i in range(nb):
                    if i:
                        c.sync()
                    x = act.activation(SQJ, B(3)[:, i * P:(i + 1) * P], ACT.Square,
                                       accum_out=ssq[:, i:i + 1])
                    if i < nb - 1:
                        c.mark(x)
                c.tell(x, sem("ssq"), T + 1)
                between()
                wait(act, sem("tkn"), T + 1)
                dst = KNT[:, 0:nb].rearrange("p a t -> p (a t)") if b < 2 else KQ[:, 0]
                act.activation(dst, B(5)[:, 0:nb * P], ACT.Copy).then_inc(sem("knt_ready"), 1)
                between()
                between()
                flat = lambda a: a[:, 0:nb].rearrange("p a t -> p (a t)")
                wait(act, sem("x_tp"), 16 * h + 6 * b + 1)
                act.activation(flat(XI), B(4)[:, 0:nb * P], ACT.Copy).then_inc(sem("xi_ready"), 1)
                for lv in range(1, (6 if b < 2 else 3) + 1):
                    wait(act, sem("w_mm"), W0 + lv)
                    act.activation(flat(WI), B(5)[:, 0:nb * P], ACT.Copy).then_inc(sem("w_ev"), 1)
                    between()
                    between()
                    if lv < 6:
                        wait(act, sem("x_tp"), 16 * h + 6 * b + 1 + lv)
                        act.activation(flat(YI), B(4)[:, 0:nb * P], ACT.Copy).then_inc(sem("y_ev"), 1)
                        between()
                for i in range(nb):
                    cc = 9 * h + 4 * b + i
                    if b == 2:
                        between()
                    wait(act, sem("qs_mm"), cc + 1)
                    if not (isinstance(h, int) and h == 0 and b == 0 and i == 0):
                        wait(act, sem("o_ready"), cc)
                    act.activation(QE, B(7)[:, 0:P], ACT.Copy, scale=HC[:, 1, 4 * b + i:4 * b + i + 1]
                                   ).then_inc(sem("qe_ready"), 1)
                    between()
                    between()
                    wait(act, sem("o_ready"), cc + 1)
                    if i == 0:
                        wait(act, sem("ssq"), T + 1)
                    else:
                        c.sync()
                    x = act.activation(SQJ, OO[:, i], ACT.Square, accum_out=sso[:, i:i + 1])
                    if i < nb - 1:
                        c.mark(x)
                    else:
                        c.tell(x, sem("sso"), T + 1)
                    between()
                between()
                between()
                assert not list(place)

            def head(h, ahead=True):
                for b in range(3):
                    if b == 0:
                        if not (isinstance(h, int) and h == 0):
                            wait(act, sem("sso"), 3 * h)
                    else:
                        wait(act, sem("sso"), 3 * h + b)
                    delta(h, b, ahead)

            for g in range(GROUPS):
                leave(0, g)
            for m in range(3):
                silu_tanh(0, m)
            tiles(act, c, H - 1, head)
            head(H - 1, False)
            act.wait_ge(sem("wout1_in"), 16)
            tiles(act, c, NT, lambda t: out(t + NT, oj1))

        @block.vector
        def _(dve):
            c = Count(dve, sem("dve_own"))
            PASSED[dve.engine] = sem("dve_passed")
            dve.wait_ge(sem("c_th"), 1)
            c.mark(dve.scalar_tensor_tensor(ctmp, ctmp, 1.0, cT, ALU.add, ALU.mult))
            c.sync()
            dve.tensor_scalar(scT, ctmp, 0.5, None, ALU.mult).then_inc(sem("sc_ready"), 1)

            def mod(l):
                dve.wait_ge(sem("mod_mm"), KT * (l + 1))
                dve.wait_ge(sem("modb_in"), 48 * (l + 1))
                for n in range(6):
                    r = slice(n * 512, (n + 1) * 512)
                    c.mark(dve.tensor_tensor(modrow[0:9, r], B(n)[0:9], modb[0:9, r], ALU.add))
                c.sync()
                dve.tensor_tensor(modrow[0:9, 2 * D:], modrow[0:9, 2 * D:], npost[0:9], ALU.mult
                                  ).then_inc(sem("mod_row"), 1)
                dve.wait_ge(sem("mod_tr"), l + 1)
                c.mark(dve.tensor_copy(modT.rearrange("p a b -> p (a b)"), B(6)[:, 0:144]))
                c.sync()
                c.mark(dve.tensor_scalar(modT[:, KT:], modT[:, KT:], 1.0, None, ALU.add))
                c.sync()
                c.mark(dve.tensor_tensor(modT[:, KT:], modT[:, KT:], bc(npre[:, l], 2, 9), ALU.mult))
                c.mark(dve.tensor_copy(gate[:, 0], psum[:, 0:2].rearrange("p a b -> p (a b)")))
                dve.tensor_copy(gate[:, 1], psum[:, 2:4].rearrange("p a b -> p (a b)")
                                ).then_inc(sem("mod_done"), 1)
                dve.wait_ge(sem("mod_done"), l + 1)

            def norm(T, t, sample):
                dve.wait_ge(sem("n_tp"), T + 1)
                src = [B(6 + k // 4)[:, (k % 4) * P:(k % 4 + 1) * P] for k in range(KT)]
                if not sample:
                    for k in range(KT):
                        i = dve.tensor_scalar(HT[:, k, bass.ds(t * P, P)], src[k],
                                              modT[:, KT + k, 0:1], modT[:, k, 0:1], ALU.mult, ALU.add)
                        if k < KT - 1:
                            c.mark(i)
                else:
                    sq = lambda a: a.rearrange("p (s u) -> p s u", s=NS)
                    for k in range(KT):
                        c.mark(dve.tensor_tensor(sq(HT[:, k, SEQ:]), sq(src[k]),
                                                 bc(modT[:, KT + k, 1:], 2, DS), ALU.mult))
                    c.sync()
                    for k in range(KT):
                        i = dve.tensor_tensor(sq(HT[:, k, SEQ:]), sq(HT[:, k, SEQ:]),
                                              bc(modT[:, k, 1:], 2, DS), ALU.add)
                i.then_inc(sem("n_ev"), 1)

            mod(0)
            tiles(dve, c, NT - 1, lambda t: norm(t, t, False))
            norm(NT - 1, NT - 1, True)

            dve.wait_ge(sem("sp_ln"), 1)
            c.mark(dve.tensor_scalar(ltmp[:, 3], lam, -1.0, 0.0, ALU.mult, ALU.max))
            c.mark(dve.tensor_scalar(gbias, gbias, 0.5, None, ALU.mult))
            c.sync()
            c.mark(dve.tensor_tensor(ltmp[:, 3], ltmp[:, 3], ltmp[:, 2], ALU.add))
            c.sync()
            c.mark(dve.tensor_scalar(kneg, ltmp[:, 3], 4.0, None, ALU.mult))
            dve.tensor_scalar(ksp, ltmp[:, 3], -4.0, None, ALU.mult).then_inc(sem("l_const"), 1)
            dve.wait_ge(sem("ua_zero"), 1)

            def lru(m):
                first = isinstance(m, int) and m == 0
                one = bass.ds(m, 1)
                if first:
                    dve.wait_ge(sem("xa_ev"), 12)
                else:
                    dve.wait_ge(sem("l_y"), m)
                c.sync()
                u = lambda j: UA[:, one, j:j + UC].rearrange("p a u -> p (a u)")
                w = lambda j: cw0[:, one, j]
                c.mark(dve.tensor_scalar(cv, u(0), w(0), w(TAPS), ALU.mult, ALU.add))
                c.sync()
                for j in (1, 2):
                    c.mark(dve.scalar_tensor_tensor(cv, u(j), w(j), cv, ALU.mult, ALU.add))
                    c.sync()
                c.mark(dve.scalar_tensor_tensor(xc[:, 0:SEQ], u(3)[:, 0:SEQ], w(3), cv[:, 0:SEQ],
                                                ALU.mult, ALU.add))
                us = UA[:, one, US:].rearrange("p a (s u) -> p (a s) u", s=NS)[:, :, PRE:]
                cs = cv_row[:, US:].rearrange("p (s u) -> p s u", s=NS)[:, :, 0:DS]
                dve.scalar_tensor_tensor(xc[:, SEQ:].rearrange("p (s u) -> p s u", s=NS), us, w(3), cs,
                                         ALU.mult, ALU.add).then_inc(sem("xc_ready"), 1)
                for g in range(6):
                    dve.wait_ge(sem("g_th"), 6 * m + g + 1)
                    row = m if g < 3 else m + 4
                    dst = YT[:, bass.ds(row, 1), (g % 3) * NC:(g % 3 + 1) * NC].rearrange("p a t -> p (a t)")
                    dve.scalar_tensor_tensor(dst, th[:, g % 2], 1.0, B(g)[:, 0:NC], ALU.add, ALU.mult
                                             ).then_inc(sem("g_ev"), 1)
                dve.wait_ge(sem("l_a"), m + 1)
                dve.wait_ge(sem("lz_ev"), 6 * m + 6)
                c.mark(dve.tensor_tensor(lg, la, la, ALU.mult))
                c.sync()
                dve.scalar_tensor_tensor(lw_, lg, 1.0, lw_, ALU.add, ALU.mult).then_inc(sem("l_w"), 1)
                c.mark(dve.scalar_tensor_tensor(ti, ti, 1.0, xc, ALU.add, ALU.mult))
                dve.wait_ge(sem("l_sq"), m + 1)
                c.sync()
                c.mark(dve.scalar_tensor_tensor(lg, ti, 0.5, lw_, ALU.mult, ALU.mult))
                c.sync()
                c.mark(dve.tensor_tensor_scan(lh[:, 0:SEQ], la[:, 0:SEQ], lg[:, 0:SEQ], 0.0,
                                              ALU.mult, ALU.add))
                for s in range(NS):
                    r = slice(SEQ + s * DS, SEQ + (s + 1) * DS)
                    c.mark(dve.tensor_tensor_scan(lh[:, r], la[:, r], lg[:, r], h0[:, one, s],
                                                  ALU.mult, ALU.add))
                c.sync()
                c.mark(dve.tensor_copy(hc[:, one, 0], lh[:, SEQ - 1:SEQ]))
                c.mark(dve.tensor_copy(hc[:, one, 1:].rearrange("p a s -> p (a s)"),
                                       lh[:, SEQ + DS - 1:TOK:DS]))
                y = YT[:, one, :].rearrange("p a t -> p (a t)")
                dve.wait_ge(sem("g_ev"), 6 * m + 3)
                dve.scalar_tensor_tensor(y, lh, 0.5, y, ALU.mult, ALU.mult).then_inc(sem("l_y"), 1)

            tiles(dve, c, LM, lru)
            dve.wait_ge(sem("att_in"), 16 * 7)

            def rot(t):
                dve.wait_ge(sem("qkv_ev"), t + 1)
                cs = rope[:, bass.ds(t, 1), 0:16].rearrange("p a r -> p (a r)")
                sn = rope[:, bass.ds(t, 1), 16:32].rearrange("p a r -> p (a r)")
                c.mark(dve.tensor_tensor(ra, QK[:, :, 0:16], bc(cs, 1, 10), ALU.mult))
                c.mark(dve.tensor_tensor(rb[:, :, 0:8], QK[:, :, 8:16], bc(sn[:, 0:8], 1, 10), ALU.mult))
                c.mark(dve.tensor_tensor(rb[:, :, 8:16], QK[:, :, 0:8], bc(sn[:, 8:16], 1, 10), ALU.mult))
                c.sync()
                dve.tensor_tensor(QK[:, :, 0:16], ra, rb, ALU.add).then_inc(sem("rope_done"), 1)

            def att(t):
                first = isinstance(t, int) and t == 0
                sample = isinstance(t, int) and t == NT - 1
                for u in range(4):
                    dve.wait_ge(sem("s_mm"), 4 * t + u + 1)
                    if not first:
                        wait(dve, sem("pt_tp"), 4 * t + u - 3)
                    for a in range(2):
                        n = 2 * u + a
                        mask = smask[:, n] if sample else amask[:, 0 if first else 1]
                        i = dve.tensor_tensor_reduce(SS[:, n], B(4 + u % 2)[:, a * 256:(a + 1) * 256],
                                                     mask, 1.0, -3.0e38, ALU.add, ALU.max, mx[:, n:n + 1])
                        if a == 0:
                            c.mark(i)
                    i.then_inc(sem("s_add"), 1)
                sink = sinkS.broadcast_to([P, 8]) if sample else sinkP
                dve.wait_ge(sem("s_add"), 4 * t + 4)
                c.mark(dve.scalar_tensor_tensor(m2, mx, HD ** -0.5, sink, ALU.mult, ALU.max))
                c.sync()
                c.mark(dve.tensor_tensor(es, sink, m2, ALU.subtract))
                dve.tensor_scalar(nm, m2, -1.0, None, ALU.mult).then_inc(sem("s_stat"), 1)
                dve.wait_ge(sem("p_exp"), t + 1)
                c.mark(dve.tensor_tensor(d2, den, es, ALU.add))
                c.sync()
                c.mark(dve.reciprocal(rd, d2))
                c.sync()
                for u in range(4):
                    for a in range(2):
                        n = 2 * u + a
                        i = dve.tensor_scalar(SS[:, n], SS[:, n], rd[:, n:n + 1], None, ALU.mult)
                        if a == 0:
                            c.mark(i)
                    i.then_inc(sem("p_norm"), 1)
                if not sample:
                    rot(t + 1)
                dve.wait_ge(sem("pv_mm"), 4 * t + 4)
                if sample:
                    for j in range(4):
                        o = B(3).rearrange("p (s j u) -> p j s u", s=NS, j=4)[:, j]
                        y = YT[:, 4 + j, SEQ:].rearrange("p (s u) -> p s u", s=NS)
                        i = dve.scalar_tensor_tensor(y, o, 0.5, y, ALU.mult, ALU.mult)
                        if j < 3:
                            c.mark(i)
                    i.then_inc(sem("o_ev"), 1)
                else:
                    y = YT[:, 4:8, bass.ds(t * P, P)]
                    dve.scalar_tensor_tensor(y, B(3).rearrange("p (j u) -> p j u", j=4), 0.5, y,
                                             ALU.mult, ALU.mult).then_inc(sem("o_ev"), 1)

            rot(0)
            tiles(dve, c, 7, att)
            att(7)
            att(8)
            def out(T, x, tmp, w):
                if not (isinstance(T, int) and T == 0):
                    dve.wait_ge(sem("x1_done"), T)
                dve.wait_ge(sem("o_rs"), T + 1)
                c.mark(dve.scalar_tensor_tensor(tmp[:, 0:512], B(0), stat[:, 8:9], gate[:, w, 0:512],
                                                ALU.mult, ALU.mult))
                dve.scalar_tensor_tensor(tmp[:, 512:], B(1), stat[:, 8:9], gate[:, w, 512:],
                                         ALU.mult, ALU.mult).then_inc(sem("out_ev"), 1)
                dve.wait_ge(sem("out_ev"), T + 1)
                dve.tensor_tensor(x, x, tmp, ALU.add).then_inc(sem("x1_done"), 1)

            row = lambda t: X[:, bass.ds(t, 1)].rearrange("p a d -> p (a d)")
            tiles(dve, c, NT - 1, lambda t: out(t, row(t), otmp, 0))
            out(NT - 1, row(NT - 1), otmp, 1)
            dve.wait_ge(sem("x1_done"), NT)
            mod(1)
            tiles(dve, c, NT - 1, lambda t: norm(t + NT, t, False))
            norm(2 * NT - 1, NT - 1, True)

            dve.wait_ge(sem("ba_ln"), 1)
            c.mark(dve.scalar_tensor_tensor(Z2[0:H], Z[0:H], 0.0, Z1[0:H], ALU.max, ALU.add))
            c.sync()
            c.mark(dve.tensor_scalar(Z[0:H, 1], Z2[0:H, 1], nega[0:H], -1.0, ALU.mult, ALU.mult))
            c.sync()
            c.mark(dve.tensor_tensor_scan(GR[0:H, 1], reset[0:H], Z[0:H, 1], 0.0, ALU.mult, ALU.add))
            c.sync()
            c.mark(dve.tensor_tensor(GR[0:H, 0], GR[0:H, 1], Z2[0:H, 0], ALU.subtract))
            c.mark(dve.tensor_copy(GL[0:H, 0:8], GR[0:H, 1, P - 1:SEQ:P]))
            c.mark(dve.tensor_copy(GL[0:H, 8:16], GR[0:H, 1, SEQ + DS - 1:TOK:DS]))
            c.sync()
            c.mark(dve.tensor_tensor(GR[0:H, 2, 0:SEQ].rearrange("p (c t) -> p c t", t=P),
                                     bc(GL[0:H, 0:8], 2, P),
                                     GR[0:H, 1, 0:SEQ].rearrange("p (c t) -> p c t", t=P), ALU.subtract))
            dve.tensor_tensor(GR[0:H, 2, SEQ:].rearrange("p (c t) -> p c t", t=DS),
                              bc(GL[0:H, 8:16], 2, DS),
                              GR[0:H, 1, SEQ:].rearrange("p (c t) -> p c t", t=DS), ALU.subtract
                              ).then_inc(sem("gl_ready"), 1)
            dve.wait_ge(sem("col_tr"), 1)
            tr3 = B(3)[:, 0:3 * NT * H].rearrange("p (q t h) -> p q t h", q=3, t=NT)
            c.mark(dve.tensor_copy(CA[:, 0], tr3[:, 1]))
            c.mark(dve.tensor_copy(CA[:, 1], tr3[:, 1]))
            c.mark(dve.tensor_copy(CA[:, 3], tr3[:, 0]))
            c.mark(dve.tensor_copy(CA[:, 4], tr3[:, 2]))
            c.sync()
            dve.tensor_tensor(CA[:, 2], CA[:, 3], CA[:, 0], ALU.subtract).then_inc(sem("ca_arg"), 1)
            dve.wait_ge(sem("ca_exp"), 1)
            c.mark(dve.tensor_scalar(CA[:, 2], CA[:, 2], 0.5, None, ALU.mult))
            c.mark(dve.tensor_scalar(CA[:, 3], CA[:, 3], -1.0, None, ALU.mult))
            dve.wait_ge(sem("l1_in"), 16 * 6)
            c.mark(dve.tensor_scalar(HN, HN, 0.5, None, ALU.mult))
            dve.wait_ge(sem("u1_zero"), 1)
            dve.wait_ge(sem("rows_out"), 48)
            c.sync()

            def conv(h, g, j):
                m, n = divmod(g, 3)
                lo, hi = n * NC, (n + 1) * NC if n < 2 else UC
                w = CW[:, bass.ds(h * 3 + m, 1), j]
                cvm = CV[:, m, lo:hi]
                if j == 0:
                    dve.wait_ge(sem("pj_ev"), 9 * h + g + 1)
                    if n == 2:
                        dve.wait_ge(sem("cs_in"), 48 * h + 48)
                    if n == 0 and not (isinstance(h, int) and h == 0):
                        dve.wait_ge(sem("s1_ready"), 3 * h)
                    c.mark(dve.tensor_scalar(cvm, U1[:, m, lo:hi], w, None, ALU.mult))
                else:
                    c.sync()
                    x = dve.scalar_tensor_tensor(cvm, U1[:, m, lo + j:hi + j], w, cvm, ALU.mult, ALU.add)
                    if n == 2 and j == PRE:
                        c.tell(x, sem("cv_done"), 3 * h + m + 1)
                    else:
                        c.mark(x)

            def gated(h, n):
                dve.wait_ge(sem("z_th"), 3 * h + n + 1)
                y = YT[:, bass.ds(h, 1), n * NC:(n + 1) * NC].rearrange("p a t -> p (a t)")
                dve.scalar_tensor_tensor(y, zt[:, n % 2], 1.0, B((9 + n) % 2)[:, 0:NC], ALU.add, ALU.mult
                                         ).then_inc(sem("z_ev"), 1)

            def silu(h, m):
                dve.wait_ge(sem("th1"), 3 * h + m + 1)
                if not (isinstance(h, int) and h == 0):
                    dve.wait_ge(sem("gq_mm"), 3 * h)
                    dve.wait_ge(sem("kq_ready"), h)
                c.mark(dve.scalar_tensor_tensor(S1[:, m, 0:SEQ], TH1[:, 0:SEQ], 1.0, CV[:, m, 0:SEQ],
                                                ALU.add, ALU.mult))
                sm = lambda a: a.rearrange("p (s u) -> p s u", s=NS)[:, :, 0:DS]
                c.tell(dve.scalar_tensor_tensor(S1[:, m, SEQ:].rearrange("p (s u) -> p s u", s=NS),
                                                sm(TH1[:, US:]), 1.0, sm(CV[:, m, US:]),
                                                ALU.add, ALU.mult), sem("s1_ready"), 3 * h + m + 1)

            def delta(h, b, ahead):
                nb = 4 if b < 2 else 1
                T = 3 * h + b
                W0 = 15 * h + 6 * b
                b4 = lambda bk: B(bk)[:, 0:nb * P].rearrange("p (a t) -> p a t", t=P)
                place = iter(range(len(PLACES[b])))

                def between():
                    p = next(place)
                    if not ahead:
                        return
                    for g in ended(b, p):
                        if g >= GB:
                            gated(h + 1, g - GB)
                    for j in range(TAPS):
                        for g in ended_before(b, p, 1 + j):
                            if g < GB:
                                conv(h + 1, g, j)
                    if b == 2 and p in (4, 7, 10):
                        silu(h + 1, (p - 4) // 3)

                if b == 0:
                    dve.wait_ge(sem("s1_ready"), 3 * h + 3)
                    if not (isinstance(h, int) and h == 0):
                        dve.wait_ge(sem("sp_out"), 16 * h)
                        dve.wait_ge(sem("y1_done"), 3 * h)
                    c.mark(dve.tensor_copy(HC, CA[:, :, :, bass.ds(h, 1)].rearrange("p q t a -> p q (t a)")))
                    c.sync()
                    dve.memset(SP, 0.0).then_inc(sem("st_ready"), 1)
                    dve.wait_ge(sem("rowb_in"), 16 * h + 16)
                else:
                    dve.wait_ge(sem("y1_done"), T)
                for q, E in ((0, EA), (1, EQ)):
                    for i in range(nb):
                        k = 4 * b + i
                        x = dve.scalar_tensor_tensor(E[:, i], rowb[:, q, k * P:(k + 1) * P],
                                                     HC[:, 0, k:k + 1], MU[:, b // 2, q],
                                                     ALU.subtract, ALU.min)
                        if q == 0 or i < nb - 1:
                            c.mark(x)
                x.then_inc(sem("e_arg"), 1)
                dve.wait_ge(sem("rk_ready"), T + 1)
                dve.tensor_tensor(KN[:, 0:nb], b4(2), bc(rk[:, 0:nb], 2, P), ALU.mult
                                  ).then_inc(sem("kn_ready"), 1)
                dve.wait_ge(sem("tv"), T + 1)
                dve.tensor_tensor(VB[:, 0:nb], b4(4), bc(HC[:, 2, 4 * b:4 * b + nb], 2, P), ALU.mult
                                  ).then_inc(sem("vb_ready"), 1)
                between()
                between()
                dve.wait_ge(sem("gq_mm"), T + 1)
                dve.wait_ge(sem("e_exp"), T + 1)
                c.tell(dve.tensor_tensor(UM[:, 0:nb], b4(2), EA[:, 0:nb], ALU.mult),
                       sem("um_ready"), T + 1)
                dve.tensor_tensor(EQ[:, 0:nb], b4(3), EQ[:, 0:nb], ALU.mult
                                  ).then_inc(sem("qkt_ready"), 1)
                dve.wait_ge(sem("lv_ready"), 18 * h + 7 * b + 1)
                dve.tensor_tensor(YI[:, 0:nb], bc(ident, 1, nb), LV[:, 0, 0:nb], ALU.subtract
                                  ).then_inc(sem("y0_ready"), 1)
                between()
                for lv in range(1, (6 if b < 2 else 3) + 1):
                    between()
                    dve.wait_ge(sem("n_mm"), W0 + lv)
                    dst = XI if lv < 6 else YI
                    if lv == 1:
                        dve.wait_ge(sem("xi_ready"), T + 1)
                    else:
                        dve.wait_ge(sem("n_ev1"), W0 + lv - 1)
                    if lv == 6:
                        dve.wait_ge(sem("y_ev"), 13 * h + 5 * b + 5)
                    dve.tensor_tensor(dst[:, 0:nb], dst[:, 0:nb], b4(2), ALU.subtract
                                      ).then_inc(sem("n_ev1"), 1)
                    between()
                    if lv < 6:
                        between()
                if b == 2:
                    dve.wait_ge(sem("kqs_mm"), h + 1)
                    dve.tensor_copy(KQS.rearrange("p a (s u) -> p a s u", s=NS),
                                    B(6)[:, 0:256].rearrange("p (s a u) -> p a s u", s=NS, a=2)
                                    ).then_inc(sem("kqs_ev"), 1)
                    between()
                for i in range(nb):
                    k = 4 * b + i
                    cc = 9 * h + k
                    dve.wait_ge(sem("ks_mm"), cc + 1)
                    dve.wait_ge(sem("vb_ready"), T + 1)
                    dve.scalar_tensor_tensor(RR, B(6)[:, 0:P], HC[:, 3, k:k + 1], VB[:, i],
                                             ALU.mult, ALU.add).then_inc(sem("r_ready"), 1)
                    between()
                    dve.wait_ge(sem("tr_mm"), cc + 1)
                    dve.tensor_copy(VN, B(6)[:, P:2 * P]).then_inc(sem("vn_ready"), 1)
                    between()
                    if b < 2:
                        dve.wait_ge(sem("kv_mm"), 8 * h + k + 1)
                        if k:
                            dve.wait_ge(sem("st_ready"), cc + 1)
                        dve.scalar_tensor_tensor(SP, SP, EG[:, bass.ds(h, 1), k], B(6)[:, 2 * P:3 * P],
                                                 ALU.mult, ALU.add).then_inc(sem("st_ready"), 1)
                    else:
                        dve.wait_ge(sem("vn_ready"), cc + 1)
                        dve.tensor_tensor(VM, bc(VN, 1, NS), bc(M8, 2, P), ALU.mult
                                          ).then_inc(sem("vm_ready"), 1)
                    dve.wait_ge(sem("o_mm"), cc + 1)
                    dve.tensor_tensor(OO[:, i], QE, B(7)[:, P:2 * P], ALU.add
                                      ).then_inc(sem("o_ready"), 1)
                    between()
                if b == 2:
                    dve.wait_ge(sem("skv_mm"), h + 1)
                    c.mark(dve.tensor_tensor(
                        SS1, SS1, bc(EG[:, bass.ds(h, 1), 8:16].rearrange("p a s -> p (a s)"), 2, P),
                        ALU.mult))
                    c.sync()
                    dve.tensor_tensor(SS1.rearrange("p s v -> p (s v)"), SS1.rearrange("p s v -> p (s v)"),
                                      psum[:, 4:6].rearrange("p a b -> p (a b)"), ALU.add
                                      ).then_inc(sem("ss_ready"), 1)
                dve.wait_ge(sem("fo_ready"), T + 1)
                dve.wait_ge(sem("o_ready"), 9 * h + 4 * b + nb)
                dve.tensor_tensor(ON[:, 0:nb], OO[:, 0:nb], bc(fo[:, 0:nb], 2, P), ALU.mult
                                  ).then_inc(sem("on_ready"), 1)
                between()
                dve.wait_ge(sem("o_tp"), T + 1)
                dve.wait_ge(sem("z_ev"), 3 * h + 3)
                y = YT[:, bass.ds(h, 1), 4 * b * P:(4 * b + nb) * P].rearrange("p a t -> p (a t)")
                dve.scalar_tensor_tensor(y, B(2)[:, 0:nb * P], HN, y, ALU.mult, ALU.mult
                                         ).then_inc(sem("y1_done"), 1)
                between()
                assert not list(place)

            def head(h, ahead=True):
                for b in range(3):
                    delta(h, b, ahead)

            for g in range(GROUPS):
                if g < GB:
                    for j in range(TAPS):
                        conv(0, g, j)
                else:
                    gated(0, g - GB)
            for m in range(3):
                silu(0, m)
            tiles(dve, c, H - 1, head)
            head(H - 1, False)

            def last(t, w):
                dve.wait_ge(sem("xt_in"), 16 * t + 16)
                out(t + NT, XT[:, 0], otmp1, w)

            tiles(dve, c, NT - 1, lambda t: last(t, 0))
            last(NT - 1, 1)


def _rows(w):
    return np.ascontiguousarray(w.reshape(KT, P, -1).transpose(1, 0, 2))


def _cols(v):
    return np.ascontiguousarray(v.reshape(-1, P).T)


def _shape_constants():
    c = {"ident": np.eye(P, dtype=np.float32)}
    sel = np.zeros((9, 2, P), np.float32)
    sel[0, 0] = 1
    for s in range(NS):
        sel[1 + s, 1, s * DS:(s + 1) * DS] = 1
    c["sel"] = sel
    am = np.zeros((P, 2, 2 * WIN), np.float32)
    am[:64, :, 192:] = NEG
    am[64:, :, :64] = NEG
    am[:, 0, :WIN] = NEG
    c["amask"] = am
    sm = np.full((NS, 2 * WIN), NEG, np.float32)
    sm[:, :WIN] = 0
    for s in range(NS):
        sm[s, WIN + s * DS:WIN + (s + 1) * DS] = 0
    c["smask"] = sm.reshape(1, -1)
    pos = np.concatenate([np.arange(SEQ), np.tile(1024 + np.arange(DS), NS)]).astype(np.float32)
    inv = (500000.0 ** (-(np.arange(8, dtype=np.float32) * 2.0 / 16))).astype(np.float32)
    ang = pos[:, None] * inv[None, :]
    co, si = np.cos(ang).astype(np.float32), np.sin(ang).astype(np.float32)
    r = np.concatenate([co, co, -si, si], 1)
    c["rope"] = np.ascontiguousarray(r.reshape(NT, P, 32).transpose(1, 0, 2))
    j, i = np.arange(P)[:, None], np.arange(P)[None, :]
    mu = np.full((P, 2, 2, P), NEG, np.float32)
    for w, same in enumerate((j >= 0, j // DS == i // DS)):
        mu[:, w, 0][(i > j) & same] = 0
        mu[:, w, 1][(i >= j) & same] = 0
    c["maskU"] = mu
    lm = np.zeros((P, 7, P), np.float32)
    for lv in range(7):
        n = 1 << lv
        lm[:, lv] = (j // (2 * n) == i // (2 * n)) & ((j // n) % 2 == 0) & ((i // n) % 2 == 1)
    c["lmask"] = lm
    c["mask8"] = (np.arange(P)[:, None] // DS == np.arange(NS)[None, :]).astype(np.float32)
    r = np.ones((H, TOK), np.float32)
    r[:, 0:SEQ:P] = 0
    r[:, SEQ::DS] = 0
    c["reset"] = r
    return c


def _lay_out(a):
    d = _shape_constants()
    x = np.concatenate([a["x_prompt"].reshape(SEQ, D), a["x_sample"].reshape(P, D)])
    d["x"] = np.ascontiguousarray(x.reshape(NT, P, D).transpose(1, 0, 2))
    cc = np.concatenate([a["c_prompt"], a["c_sample"]])
    d["cT"] = np.ascontiguousarray(cc.T.reshape(KT, P, 9).transpose(1, 0, 2))
    d["modw"] = np.stack([a["ev_mod_w"][0], a["od_mod_w"][0]]).reshape(2, KT, P, 3 * D)
    d["modb"] = np.stack([a["ev_mod_b"][0], a["od_mod_b"][0]])
    d["npre"] = np.stack([_cols(a["ev_norm_pre"][0]), _cols(a["od_norm_pre"][0])], 1)
    d["npost"] = np.stack([a["ev_norm_post"][0], a["od_norm_post"][0]])
    w = a["ev_w_in"][0]
    pair = np.concatenate([np.r_[HD * j:HD * j + HD, HD * (j + 4):HD * (j + 4) + HD] for j in range(4)])
    xa, ga, gb = w[:, 0:512], w[:, 512:1024], w[:, 1792:][:, pair]
    order = [xa[:, m * P:(m + 1) * P] for m in range(4)]
    for m in range(4):
        order += [ga[:, m * P:(m + 1) * P], gb[:, m * P:(m + 1) * P]]
    d["w0"] = np.stack([_rows(o) for o in order])
    d["wqkv"] = _rows(w[:, 1024:1792])
    wo = a["ev_w_out"][0]
    wo = np.concatenate([wo[:512], wo[512:][pair]])
    d["wout"] = np.stack([_rows(wo), _rows(a["od_w_out"][0])])
    d["cw0"] = np.ascontiguousarray(np.stack(
        [_cols(a["lru_conv_w"][0, j]) for j in range(TAPS)] + [_cols(a["lru_conv_b"][0])], 2))
    d["gbias"] = np.ascontiguousarray(np.stack([_cols(a["lru_b_a"][0]), _cols(a["lru_b_x"][0])], 2))
    d["lam"] = _cols(a["lru_lambda"][0])
    g = np.zeros((LM, P, 2, P), np.float32)
    for m in range(LM):
        for q in range(2):
            b = slice(q * 64, q * 64 + 64)
            g[m, b, 0, b] = a["lru_w_a"][0, 2 * m + q]
            g[m, b, 1, b] = a["lru_w_x"][0, 2 * m + q]
    d["gw"] = g
    ch = lambda v, n: np.ascontiguousarray(
        v.reshape(*v.shape[:-1], n, P).transpose(v.ndim, v.ndim - 1, *range(v.ndim - 1)))
    d["cs0"] = ch(a["state_lru_conv"][0], LM)
    d["h0"] = ch(a["state_lru_h"][0], LM)
    d["kc"] = np.ascontiguousarray(a["cache_swa_k"][0].reshape(NS, P, P).transpose(2, 0, 1))
    d["vc"] = np.ascontiguousarray(a["cache_swa_v"][0].reshape(NS, P, P).transpose(1, 0, 2))
    d["sinkP"] = a["swa_sinks"][0].reshape(1, 8)
    d["sinkS"] = np.repeat(a["swa_sinks"][0], DS).reshape(P, 1)
    w = a["od_w_in"][0]
    w1 = w[:, :4096].reshape(D, 4, H, P).transpose(2, 1, 0, 3).reshape(4 * H, D, P)
    d["w1"] = np.ascontiguousarray(w1.reshape(4 * H, KT, P, P).transpose(0, 2, 1, 3))
    ba = np.zeros((D, 40), np.float32)
    ba[:, 0:H], ba[:, 32:40] = w[:, 4096:4104], w[:, 4104:4112]
    d["wba"] = _rows(ba)
    d["alog"], d["dtb"] = a["gdn_a_log"].reshape(H, 1), a["gdn_dt_bias"].reshape(H, 1)
    hm = lambda v: ch(v.reshape(*v.shape[:-1], 3, H, P).swapaxes(-3, -2).reshape(*v.shape), 3 * H)
    d["cw1"] = hm(a["gdn_conv_w"][0])
    d["cs1"] = hm(a["state_gdn_conv"][0])
    d["hn"] = a["gdn_head_norm"][0].reshape(P, 1)
    d["gs"] = np.ascontiguousarray(a["state_gdn_s"][0].transpose(1, 2, 0, 3))
    return d


_OUTS = {"y": (P, NT, D), "cb0": (P, LM, 1 + NS, PRE), "hc": (P, LM, 1 + NS), "kout": (2, P, 2, HD),
         "vout": (2, P, P), "cb1": (P, 3 * H, 1 + NS, PRE), "sp": (H, P, P), "ss": (H, P, NS, P)}


def _read_out(r):
    y = r["y"].transpose(1, 0, 2).reshape(TOK, D)
    cb0 = r["cb0"].transpose(1, 0, 2, 3).reshape(LW, 1 + NS, PRE)
    hc = r["hc"].transpose(1, 0, 2).reshape(LW, 1 + NS)
    cb1 = r["cb1"].reshape(P, H, 3, 1 + NS, PRE).transpose(3, 4, 2, 1, 0).reshape(1 + NS, PRE, 3 * D)
    k, v = r["kout"], r["vout"].reshape(2, P, 2, HD)
    outs = (y[:SEQ].reshape(1, SEQ, D), y[SEQ:].reshape(NS, DS, D),
            cb0[:, 0].T.reshape(1, 1, PRE, LW), cb0[:, 1:].transpose(1, 2, 0)[None],
            hc[:, 0].reshape(1, 1, LW), hc[:, 1:].T[None],
            k[0][None, None], k[1].reshape(1, NS, DS, 2, HD),
            v[0][None, None], v[1].reshape(1, NS, DS, 2, HD),
            cb1[0][None, None], cb1[1:][None],
            r["sp"][None, None], r["ss"].transpose(2, 0, 1, 3)[None])
    return tuple(np.ascontiguousarray(o) for o in outs)


def kernel(**inputs):
    import concourse.bacc as bacc
    from concourse.bass_utils import run_bass_kernel_spmd

    nc = bacc.Bacc("TRN2", target_bir_lowering=False, num_devices=1)
    arrays = {k: np.ascontiguousarray(v) for k, v in _lay_out(inputs).items()}
    ins = {k: nc.dram_tensor(k, v.shape, F32, kind="ExternalInput").ap() for k, v in arrays.items()}
    outs = {k: nc.dram_tensor(k, shape, F32, kind="ExternalOutput").ap() for k, shape in _OUTS.items()}
    encoder(nc, ins, outs)
    r = run_bass_kernel_spmd(nc, [arrays], core_ids=[0])
    return _read_out(r.results[0])
```

```python
from contextlib import ExitStack

import numpy as np
import concourse.bass as bass
from concourse import mybir

F32 = mybir.dt.float32
ALU = mybir.AluOpType
ACT = mybir.ActivationFunctionType
AX = mybir.AxisListType

P = 128
D = 1024
KT = D // P
SEQ, NS, DS = 1024, 8, 16
NT = SEQ // P + 1
TOK = NT * P
NC = TOK // 3
LW = 512
LM = LW // P
H = 8
HD = 64
TAPS = 4
PRE = TAPS - 1
UW = PRE + SEQ + NS * (PRE + DS)
UC = UW - PRE
US = PRE + SEQ
EPS = 1e-6
NEG = -1e30
WIN = 128


def wait(eng, sem, value):
    eng.wait_ge(sem, value)
    if not isinstance(value, int):
        eng.sem_inc(PASSED[eng.engine], 1)


PASSED = {}

BA_GROUPS = 4
GROUPS, GB = 12, 9


def _places():
    plan = []
    for batches, levels, steps, lo, hi, (start, level, step, end) in (
            (2, 6, 12, 0, 8 * GB, ([12, 4, 8], [6, 6, 0], 4, [8, 4])),
            (1, 3, 4, 8 * GB, 8 * GROUPS, ([4, 2, 4], [1, 1, 0], 1, [3, 1]))):
        weights = (start + (level * levels)[:3 * levels - (levels == 6)] + [step] * steps + end) * batches
        ends = [lo + (hi - lo) * sum(weights[:i + 1]) // sum(weights) for i in range(len(weights))]
        spans = list(zip([lo] + ends, ends))
        n = len(spans) // batches
        plan += [spans[i * n:(i + 1) * n] for i in range(batches)]
    return plan


PLACES = _places()


def ended(b, place):
    lo, hi = PLACES[b][place]
    return [g for g in range(GROUPS) if lo < 8 * g + 8 <= hi]


def ended_before(b, place, back):
    while place < back:
        if b == 0:
            return []
        b -= 1
        place += len(PLACES[b])
    return ended(b, place - back)


class Count:

    def __init__(self, eng, sem):
        self.eng, self.sem, self.n, self.base = eng, sem, 0, 0
        self.last = sem, 0

    def mark(self, ins):
        self.n += 1
        self.last = self.sem, self.base + self.n
        return ins.then_inc(self.sem, 1)

    def tell(self, ins, sem, value):
        self.last = sem, value
        return ins.then_inc(sem, 1)

    def sync(self):
        wait(self.eng, *self.last)


def tiles(eng, count, n, body):
    c0 = count.n if count else 0
    body(0)
    if count:
        per = count.n - c0
    with eng.Fori(1, n) as i:
        if count:
            count.base = (i - 1) * per
        body(i)
    if count:
        count.base = 0
        count.n = c0 + n * per


def nine(eng, count, body):
    c0 = count.n if count else 0
    body(0, 0, 0)
    per = count.n - c0 if count else 0
    body(1, 1, 0)
    body(2, 0, 1)
    with eng.Fori(1, 3) as i:
        if count:
            count.base = (i - 1) * (2 * per)
        body(i * 2 + 1, 1, i)
        body(i * 2 + 2, 0, i + 1)
    if count:
        count.base = 0
        count.n = c0 + 7 * per
    body(7, 1, 3)
    body(8, 0, 4)


def past(t, n):
    return not isinstance(t, int) or t >= n


def bc(ap, axis, n):
    a = ap.unsqueeze(axis)
    shape = list(a.shape)
    shape[axis] = n
    return a.broadcast_to(shape)


def encoder(nc, I, O):
    ctx = ExitStack()
    with ctx:
        sem_made = {}

        def sem(name):
            if name not in sem_made:
                sem_made[name] = ctx.enter_context(nc.semaphore(name))
            return sem_made[name]

        ARENA = 53100
        mem = ctx.enter_context(nc.sbuf_tensor("mem", [P, ARENA], F32))
        psum = ctx.enter_context(nc.psum_tensor("psum", [P, 8, 512], F32))
        at = [0]

        def take(*shape):
            n = int(np.prod(shape))
            ap = mem[:, at[0]:at[0] + n]
            at[0] += n
            assert at[0] <= ARENA, at[0]
            if len(shape) > 1:
                names = "abcd"[:len(shape)]
                ap = ap.rearrange(f"p ({' '.join(names)}) -> p {' '.join(names)}",
                                  **{k: s for k, s in zip(names[1:], shape[1:])})
            return ap

        HT = take(KT, TOK)
        YT = take(KT, TOK)
        ident = take(P)
        gate = take(2, D)
        modT = take(16, 9)
        npre = take(2, KT)
        cT, scT, ctmp = take(KT, 9), take(KT, 9), take(KT, 9)
        stat = take(16)
        halfneg = take(8)
        fixed_end = at[0]
        X = take(NT, D)
        x_end = at[0]

        def tok(ap, t):
            return ap[:, :, bass.ds(t * P, P)]

        wout_at = at[0]
        wout = take(KT, D)
        yst, xh = take(2, KT, P), take(2, D)
        oj, otmp = take(D), take(D)
        sel, npost = take(2, P), take(D)
        modrow, modb = take(3 * D), take(3 * D)
        mw = HT.rearrange("p k t -> p (k t)")[:, 0:2 * KT * 512].rearrange(
            "p (s k c) -> p s k c", s=2, k=KT)
        at[0] = wout_at
        wqkv = take(KT, 768)
        ring_at = at[0]
        w0 = take(2, KT, P)
        UA = take(LM, UW)
        ua_end = at[0]
        th = take(2, NC)
        cw0 = take(LM, TAPS + 1)
        gbias = take(LM, 2)
        lam, ksp, ksp2, kneg = take(LM), take(LM), take(LM), take(LM)
        ltmp = take(4, LM)
        h0, hc = take(LM, NS), take(LM, 1 + NS)
        cb0 = take(LM, 1 + NS, PRE)
        gw = take(2, P)
        cv_row = take(UW)
        cv = cv_row[:, 0:UC]
        xc, tr, ti, la, lw_, lg = (take(TOK) for _ in range(6))
        lh = cv_row[:, 0:TOK]
        lru_end = at[0]
        at[0] = ring_at
        hst = take(KT, P)
        kc, vc = take(NS, P), take(NS, P)
        amask = take(2, 2 * WIN)
        smask = take(NS, 2 * WIN)
        rope = take(NT, 32)
        sinkP, sinkS = take(8), take(1)
        assert at[0] <= ua_end
        QK, ra, rb = take(10, HD), take(10, 16), take(10, 16)
        SS = take(8, 2 * WIN)
        PT = take(2, 4, P)
        qT = take(4, P)
        kT, V = take((NT + 1) * P), take(NT + 1, P)
        kw, vw = take(2 * P), take(2, P)
        mx, m2, nm, es, den, d2, rd = (take(8) for _ in range(7))
        att_end = at[0]
        at[0] = fixed_end
        U1 = take(3, UW)
        CV = take(3, UW)
        TH1 = take(UW)
        zt = take(2, NC)
        SQJ = take(P)
        HN = take(1)
        M8 = take(NS)
        ssk, ssq, sso, rk, f1, f2, fo = (take(4) for _ in range(7))
        assert at[0] <= wout_at
        at[0] = wout_at
        wr = take(4, KT, P)
        s1_at = at[0]
        S1 = take(3, TOK)
        rowb = take(2, TOK)
        KN, KNT, KD, VB = take(4, P), take(4, P), take(4, P), take(4, P)
        EA, EQ, UM, LV = take(4, P), take(4, P), take(4, P), take(2, 4, P)
        XI, YI, WI, OO, ON = take(4, P), take(4, P), take(4, P), take(4, P), take(4, P)
        RR, VN, QE, SP = take(P), take(P), take(P), take(P)
        SS1 = take(NS, P)
        VM = take(NS, P)
        KQ = take(2, P)
        KQS = take(2, P)
        hc_at = at[0]
        HC = take(5, NT)
        CA = take(5, NT, H)
        EG = take(H, 16)
        MU = take(2, 2, P)
        LM1 = take(7, P)
        CW = take(3 * H, TAPS)
        CB1 = take(3 * H, 1 + NS, PRE)
        assert at[0] <= ARENA
        at[0] = hc_at - (3 * 2 + 3 + 1) * TOK - KT * 40 - 18
        Z, Z1, Z2, GR = take(2, TOK), take(2, TOK), take(2, TOK), take(3, TOK)
        wba = take(KT, 40)
        reset = take(TOK)
        nega, dtb, GL = take(1), take(1), take(16)
        at[0] = fixed_end
        wout1 = take(KT, D)
        at[0] = wout_at
        yst1, oj1, otmp1 = take(2, KT, P), take(D), take(D)
        at[0] = s1_at
        XT = take(2, D)
        x1_dram = nc.dram_tensor("x1_dram", (P, NT, D), F32, kind="Internal").ap()
        row_dram = nc.dram_tensor("row_dram", (H, 2, TOK), F32, kind="Internal").ap()
        eg_dram = nc.dram_tensor("eg_dram", (H, 16), F32, kind="Internal").ap()

        block = ctx.enter_context(nc.Block())
        B = lambda b: psum[:, b, :]

        def knt(b, i):
            return KNT[:, i] if b < 2 else KQ[:, 0]

        @block.sync
        def _(sp):
            PASSED[sp.engine] = sem("sp_passed")
            for ap, name in ((ident, "ident"), (cT, "cT"), (npre, "npre")):
                sp.dma_start(ap, I[name]).then_inc(sem("const_in"), 16)

            def mod_rows(l):
                sp.dma_start(sel[0:9], I["sel"]).then_inc(sem("modb_in"), 16)
                sp.dma_start(modb[0:9], I["modb"][l:l + 1, :].broadcast_to([9, 3 * D])
                             ).then_inc(sem("modb_in"), 16)
                sp.dma_start(npost[0:9], I["npost"][l:l + 1, :].broadcast_to([9, D])
                             ).then_inc(sem("modb_in"), 16)

            def mod_loads(l, n):
                if n >= 2:
                    sp.wait_ge(sem("mod_mm"), 6 * l + n - 1)
                sp.dma_start(mw[:, n % 2], I["modw"][l, n]).then_inc(sem(f"mw_in{n % 2}"), 16)

            mod_rows(0)
            for n in range(6):
                mod_loads(0, n)
            sp.dma_start(X, I["x"]).then_inc(sem("x_in"), 16)
            for c in range(2):
                sp.dma_start(w0[:, c], I["w0"][c]).then_inc(sem(f"w0_in{c}"), 16)
            sp.dma_start(wqkv, I["wqkv"]).then_inc(sem("wqkv_in"), 16)
            sp.wait_ge(sem("mod_done"), 1)
            sp.wait_ge(sem("n_tp"), NT)
            for ap, name in ((cw0, "cw0"), (gbias, "gbias"), (lam, "lam"), (h0, "h0")):
                sp.dma_start(ap, I[name]).then_inc(sem("lru_in"), 16)
            for m in range(LM):
                sp.dma_start(UA[:, m, US:].rearrange("p (s u) -> p s u", s=NS)[:, :, 0:PRE],
                             I["cs0"][:, m]).then_inc(sem("lru_in"), 16)
            for c in (2, 3):
                sp.wait_ge(sem("xa_mm"), 3 * (c - 1))
                sp.dma_start(w0[:, c % 2], I["w0"][c]).then_inc(sem(f"w0_in{c % 2}"), 16)

            def gate_loads(m):
                for q in range(2):
                    if isinstance(m, int) and m == 0:
                        sp.wait_ge(sem("xa_mm"), 3 * (3 + q))
                    else:
                        sp.wait_ge(sem("g_mm"), 6 * m + 3 * q - 3)
                    sp.dma_start(w0[:, q], I["w0"][bass.ds(m * 2 + (4 + q), 1)]
                                 .rearrange("a p k c -> p (a k) c")).then_inc(sem(f"w0_in{q}"), 16)
                if not (isinstance(m, int) and m == 0):
                    sp.wait_ge(sem("l_mm"), 6 * m)
                sp.dma_start(gw, I["gw"][bass.ds(m, 1)].rearrange("a p k c -> p (a k) c")
                             ).then_inc(sem("gw_in"), 16)

            tiles(sp, None, LM, gate_loads)
            sp.wait_ge(sem("g_mm"), 6 * LM)
            sp.wait_ge(sem("xc_ready"), LM)
            sp.wait_ge(sem("hist0"), 2 * LM)
            sp.dma_start(amask, I["amask"]).then_inc(sem("att_in"), 16)
            sp.dma_start(smask.rearrange("p s k -> p (s k)"),
                         I["smask"].broadcast_to([P, NS * 2 * WIN])).then_inc(sem("att_in"), 16)
            sp.dma_start(rope, I["rope"]).then_inc(sem("att_in"), 16)
            sp.dma_start(kc, I["kc"]).then_inc(sem("att_in"), 16)
            sp.dma_start(vc, I["vc"]).then_inc(sem("att_in"), 16)
            sp.dma_start(sinkP, I["sinkP"].broadcast_to([P, 8])).then_inc(sem("att_in"), 16)
            sp.dma_start(sinkS, I["sinkS"]).then_inc(sem("att_in"), 16)
            sp.dma_start(O["cb0"], cb0).then_inc(sem("out0"), 16)
            sp.wait_ge(sem("l_y"), LM)
            sp.dma_start(O["hc"], hc).then_inc(sem("out0"), 16)
            for q, t in enumerate((7, 8)):
                sp.wait_ge(sem("rope_done"), t + 1)
                sp.dma_start(O["kout"][q], QK[:, 8:10]).then_inc(sem("kout"), 16)
            for q, t in enumerate((7, 8)):
                sp.dma_start(O["vout"][q], V[:, t + 1]).then_inc(sem("out0"), 16)
            sp.wait_ge(sem("qkv_mm"), NT)
            wo_d = 6
            sp.dma_start(wout[:, 0:wo_d], I["wout"][0, :, 0:wo_d]).then_inc(sem("wout_in"), 16)
            mod_loads(1, 0)
            mod_loads(1, 1)
            sp.wait_ge(sem("o_ev"), NT)
            sp.wait_ge(sem("out0"), 64)
            sp.wait_ge(sem("kout"), 32)
            sp.dma_start(wout[:, wo_d:], I["wout"][0, :, wo_d:]).then_inc(sem("wout_in"), 16)
            mod_rows(1)
            for n in range(2, 6):
                mod_loads(1, n)
            sp.wait_ge(sem("x1_done"), NT)
            sp.dma_start(x1_dram, X).then_inc(sem("x1_out"), 16)
            sp.wait_ge(sem("mod_done"), 2)
            for ap, name in ((wba, "wba"), (reset[0:H], "reset"), (nega[0:H], "alog"), (dtb[0:H], "dtb")):
                sp.dma_start(ap, I[name]).then_inc(sem("ba_in"), 16)
            def weights(h, m):
                sp.dma_start(wr[:, m], I["w1"][bass.ds(h * 4 + m, 1)]
                             .rearrange("a p k c -> p (a k) c")).then_inc(sem(f"w1_in{m}"), 16)

            def rows(h):
                sp.dma_start(rowb.rearrange("p a t -> p (a t)"),
                             row_dram[bass.ds(h, 1)].rearrange("a q t -> a (q t)")
                             .broadcast_to([P, 2 * TOK])).then_inc(sem("rowb_in"), 16)

            for m in range(4):
                weights(0, m)
            sp.wait_ge(sem("n_tp"), 2 * NT)
            sp.wait_ge(sem("x1_out"), 16)
            for ap, name in ((MU, "maskU"), (LM1, "lmask"), (M8, "mask8"), (CW, "cw1"), (HN, "hn")):
                sp.dma_start(ap, I[name]).then_inc(sem("l1_in"), 16)
            for m in range(3):
                sp.dma_start(U1[:, m, US:].rearrange("p (s u) -> p s u", s=NS)[:, :, 0:PRE],
                             I["cs1"][:, m]).then_inc(sem("cs_in"), 16)
            sp.wait_ge(sem("rows_ready"), 1)
            sp.dma_start(row_dram[:, 0], GR[0:H, 0]).then_inc(sem("rows_out"), 16)
            sp.dma_start(row_dram[:, 1], GR[0:H, 1]).then_inc(sem("rows_out"), 16)
            sp.dma_start(eg_dram, GL[0:H]).then_inc(sem("rows_out"), 16)
            sp.wait_ge(sem("rows_out"), 48)
            sp.wait_ge(sem("col_tr"), 1)
            sp.dma_start(EG.rearrange("p h g -> p (h g)"),
                         eg_dram.rearrange("(a h) g -> a (h g)", a=1).broadcast_to([P, H * 16])
                         ).then_inc(sem("l1_in"), 16)
            rows(0)
            for m in range(4):
                sp.wait_ge(sem("pj_mm"), 3 * m + 3)
                weights(1, m)

            def head(h, ahead):
                if ahead:
                    wait(sp, sem("cv_done"), 3 * h + 3)
                    wait(sp, sem("hist1"), 6 * h + 6)
                    for m in range(3):
                        sp.dma_start(U1[:, m, US:].rearrange("p (s u) -> p s u", s=NS)[:, :, 0:PRE],
                                     I["cs1"][:, bass.ds((h + 1) * 3 + m, 1)]
                                     .rearrange("p a s u -> p (a s) u")).then_inc(sem("cs_in"), 16)
                if not (isinstance(h, int) and h == 0):
                    sp.wait_ge(sem("ss_out"), 16 * h)
                sp.dma_start(SS1, I["gs"][bass.ds(h, 1)].rearrange("a p s v -> p (a s) v")
                             ).then_inc(sem("ss_in"), 16)
                if ahead > 1:
                    for m in range(3):
                        sp.wait_ge(sem("pj_mm"), 12 * h + 3 * m + 15)
                        weights(h + 2, m)
                sp.wait_ge(sem("st_ready"), 9 * h + 9)
                sp.dma_start(O["sp"][bass.ds(h, 1)].rearrange("a p v -> p (a v)"), SP
                             ).then_inc(sem("sp_out"), 16)
                if ahead:
                    sp.wait_ge(sem("e_arg"), 3 * h + 3)
                    rows(h + 1)
                if ahead > 1:
                    sp.wait_ge(sem("pj_mm"), 12 * h + 24)
                    weights(h + 2, 3)
                sp.wait_ge(sem("ss_ready"), h + 1)
                sp.dma_start(O["ss"][bass.ds(h, 1)].rearrange("a p s v -> p (a s) v"), SS1
                             ).then_inc(sem("ss_out"), 16)

            tiles(sp, None, H - 2, lambda h: head(h, 2))
            head(H - 2, 1)
            sp.wait_ge(sem("hist1"), 6 * H)
            sp.wait_ge(sem("s1_ready"), 3 * H)
            sp.wait_ge(sem("z_ev"), 3 * H)
            sp.dma_start(wout1, I["wout"][1]).then_inc(sem("wout1_in"), 16)
            sp.dma_start(O["cb1"], CB1).then_inc(sem("out1"), 16)
            head(H - 1, 0)
            sp.wait_ge(sem("y1_done"), 3 * H)

            def residual(t, slot, turn):
                if not (isinstance(turn, int) and turn == 0):
                    wait(sp, sem(f"y_out{slot}"), 16 * turn)
                sp.dma_start(XT[:, slot], x1_dram[:, bass.ds(t, 1)].rearrange("p a d -> p (a d)")
                             ).then_inc(sem(f"xt_in{slot}"), 16)

            def last(t, slot, turn):
                if not (isinstance(t, int) and t == NT - 1):
                    residual(t + 1, 1 - slot, turn + slot)
                wait(sp, sem("x1_done"), NT + t + 1)
                sp.dma_start(O["y"][:, bass.ds(t, 1)].rearrange("p a d -> p (a d)"), XT[:, slot]
                             ).then_inc(sem(f"y_out{slot}"), 16)

            residual(0, 0, 0)
            nine(sp, None, last)
            sp.wait_ge(sem("y_out0"), 16 * 5)
            sp.wait_ge(sem("y_out1"), 16 * 4)
            sp.wait_ge(sem("sp_out"), 16 * H)
            sp.wait_ge(sem("ss_out"), 16 * H)
            sp.wait_ge(sem("out1"), 16)

        @block.gpsimd
        def _(pool):
            c = Count(pool, sem("pool_own"))
            PASSED[pool.engine] = sem("pool_passed")
            c.mark(pool.memset(halfneg, -0.5))
            c.sync()

            def norm(l, t, slot):
                T = l * NT + t
                st = lambda q: stat[:, 3 * slot + q:3 * slot + q + 1]
                wait(pool, sem("n_ss"), T + 1)
                c.mark(pool.tensor_scalar(st(1), st(0), 1.0 / D, EPS, ALU.mult, ALU.add))
                c.sync()
                pool.tensor_tensor(st(2), st(1), halfneg[:, 0:1], ALU.pow).then_inc(sem("n_rs"), 1)

            nine(pool, c, lambda t, slot, turn: norm(0, t, slot))
            wait(pool, sem("n_tp"), NT)
            pool.memset(UA[:, :, 0:PRE], 0.0).then_inc(sem("ua_zero"), 1)

            def hist(m):
                if isinstance(m, int):
                    wait(pool, sem("xa_ev"), 12)
                    wait(pool, sem("lru_in"), 16 * 8)
                pool.tensor_copy(cb0[:, bass.ds(m, 1), 0], UA[:, bass.ds(m, 1), SEQ:SEQ + PRE]
                                 ).then_inc(sem("hist0"), 1)
                s = UA[:, m, US:].rearrange("p (s u) -> p s u", s=NS)[:, :, DS:]
                pool.tensor_copy(cb0[:, m, 1:], s).then_inc(sem("hist0"), 1)

            for m in range(LM):
                hist(m)
            def stage(t):
                if not (isinstance(t, int) and t == 0):
                    wait(pool, sem("qkv_mm"), t)
                pool.tensor_copy(hst, tok(HT, t)).then_inc(sem("hst_ready"), 1)

            def window(t):
                stage(t + 1)
                wait(pool, sem("qT_ev"), t + 1)
                if not (isinstance(t, int) and t == 0):
                    wait(pool, sem("s_mm"), 4 * t)
                pool.tensor_copy(kw, kT[:, bass.ds(t * P, 2 * P)]).then_inc(sem("kw_ready"), 1)
                if not (isinstance(t, int) and t == 0):
                    wait(pool, sem("pv_mm"), 4 * t)
                pool.tensor_copy(vw, V[:, bass.ds(t, 2)]).then_inc(sem("vw_ready"), 1)

            wait(pool, sem("g_mm"), 6 * LM)
            stage(0)
            wait(pool, sem("l_y"), LM)
            wait(pool, sem("out0"), 32)
            c.mark(pool.memset(kT[:, 0:P], 0.0))
            c.mark(pool.memset(V[:, 0], 0.0))
            c.sync()
            tiles(pool, None, NT - 1, window)

            def stationary(l, t, slot, stage_to):
                if l or past(t, 2):
                    wait(pool, sem("out_mm"), l * NT + t - 1)
                pool.tensor_copy(stage_to[:, slot], tok(YT, t)).then_inc(sem("yst_ready"), 1)

            def out(l, t, slot, stage_to):
                if not (isinstance(t, int) and t == NT - 1):
                    stationary(l, t + 1, 1 - slot, stage_to)
                st = lambda q: stat[:, 6 + 5 * slot + q:7 + 5 * slot + q]
                wait(pool, sem("o_ss"), l * NT + t + 1)
                c.mark(pool.tensor_tensor(st(2), st(0), st(1), ALU.add))
                c.sync()
                c.mark(pool.tensor_scalar(st(3), st(2), 1.0 / D, EPS, ALU.mult, ALU.add))
                c.sync()
                pool.tensor_tensor(st(4), st(3), halfneg[:, 0:1], ALU.pow).then_inc(sem("o_rs"), 1)

            wait(pool, sem("o_ev"), NT)
            wait(pool, sem("rope_done"), NT)
            wait(pool, sem("kout"), 32)
            wait(pool, sem("out0"), 64)
            stationary(0, 0, 0, yst)
            nine(pool, c, lambda t, slot, turn: out(0, t, slot, yst))
            nine(pool, c, lambda t, slot, turn: norm(1, t, slot))
            wait(pool, sem("n_tp"), 2 * NT)
            wait(pool, sem("x1_out"), 16)
            pool.memset(U1[:, :, 0:PRE], 0.0).then_inc(sem("u1_zero"), 1)

            def hist1(h):
                wait(pool, sem("pj_ev"), 9 * h + 9)
                wait(pool, sem("cs_in"), 48 * h + 48)
                for m in range(3):
                    pool.tensor_copy(CB1[:, bass.ds(h * 3 + m, 1), 0], U1[:, m:m + 1, SEQ:US]
                                     ).then_inc(sem("hist1"), 1)
                    pool.tensor_copy(
                        CB1[:, bass.ds(h * 3 + m, 1), 1:].rearrange("p a s u -> p (a s) u"),
                        U1[:, m, US:].rearrange("p (s u) -> p s u", s=NS)[:, :, DS:]
                    ).then_inc(sem("hist1"), 1)

            def delta(h, b):
                nb = 4 if b < 2 else 1
                T = 3 * h + b
                wait(pool, sem("ssk"), T + 1)
                c.mark(pool.tensor_scalar(rk[:, 0:nb], ssk[:, 0:nb], 4 * EPS, None, ALU.add))
                c.sync()
                c.tell(pool.tensor_tensor(rk[:, 0:nb], rk[:, 0:nb], halfneg[:, 0:nb], ALU.pow),
                       sem("rk_ready"), T + 1)
                wait(pool, sem("kn_ready"), T + 1)
                pool.tensor_tensor(KD[:, 0:nb], KN[:, 0:nb], bc(HC[:, 4, 4 * b:4 * b + nb], 2, P),
                                   ALU.mult).then_inc(sem("kd_ready"), 1)
                if b == 2:
                    wait(pool, sem("s1_ready"), 3 * h + 3)
                    pool.tensor_copy(KQ[:, 1], S1[:, 0, SEQ:]).then_inc(sem("kq_ready"), 1)
                for lv in range(7 if b < 2 else 4):
                    if lv == 0:
                        wait(pool, sem("e_exp"), T + 1)
                    elif lv == 2:
                        wait(pool, sem("um_ready"), T + 1)
                    if lv >= 2:
                        if lv == 2:
                            wait(pool, sem("y0_ready"), T + 1)
                        else:
                            wait(pool, sem("w_mm"), 15 * h + 6 * b + lv - 2)
                    pool.tensor_tensor(LV[:, lv % 2, 0:nb], (EA if lv < 2 else UM)[:, 0:nb],
                                       bc(LM1[:, lv], 1, nb),
                                       ALU.mult).then_inc(sem("lv_ready"), 1)
                wait(pool, sem("ssq"), T + 1)
                c.mark(pool.tensor_scalar(f1[:, 0:nb], ssq[:, 0:nb], P * EPS, 4 * P * EPS * EPS,
                                          ALU.mult, ALU.add))
                wait(pool, sem("sso"), T + 1)
                c.mark(pool.tensor_scalar(f2[:, 0:nb], sso[:, 0:nb], 1.0 / P, None, ALU.mult))
                c.sync()
                c.mark(pool.tensor_tensor(f2[:, 0:nb], f2[:, 0:nb], f1[:, 0:nb], ALU.add))
                c.sync()
                c.tell(pool.tensor_tensor(fo[:, 0:nb], f2[:, 0:nb], halfneg[:, 0:nb], ALU.pow),
                       sem("fo_ready"), T + 1)

            def head(h, ahead=True):
                for b in range(3):
                    delta(h, b)
                if ahead:
                    hist1(h + 1)

            hist1(0)
            tiles(pool, c, H - 1, head)
            head(H - 1, False)
            wait(pool, sem("y1_done"), 3 * H)
            wait(pool, sem("z_ev"), 3 * H)
            stationary(1, 0, 0, yst1)
            nine(pool, c, lambda t, slot, turn: out(1, t, slot, yst1))

        @block.tensor
        def _(pe):
            def mm(*a, **k):
                return pe.matmul(*a, **k)

            def tr(out, in_, n=P):
                return pe.transpose(out, in_, ident[0:n, 0:n])

            def mod_chunk(l, n, slot, turn):
                pe.wait_ge(sem(f"mw_in{slot}"), 16 * (3 * l + 1) + 16 * turn)
                if l or past(n, 2):
                    pe.wait_ge(sem("mod_ev"), 6 * l - 1 + n)
                for k in range(KT):
                    i = mm(B(4 + slot)[0:9], scT[:, k], mw[:, slot, k],
                           start=(k == 0), stop=(k == KT - 1))
                i.then_inc(sem("mod_mm"), 1)

            def mod_turn(l):
                pe.wait_ge(sem("mod_row"), l + 1)
                for j in range(16):
                    tr(B(6)[:, 9 * j:9 * j + 9], modrow[0:9, j * P:(j + 1) * P], 9)
                for w in range(2):
                    for n in range(2):
                        i = mm(B(2 * w + n), sel[0:9, w],
                               modrow[0:9, 2 * D + n * 512:2 * D + (n + 1) * 512],
                               start=True, stop=True)
                i.then_inc(sem("mod_tr"), 1)

            def norm(l, t, slot):
                pe.wait_ge(sem("n_xh"), l * NT + t + 1)
                if past(t, 2):
                    pe.wait_ge(sem("n_ev"), l * NT + t - 1)
                else:
                    pe.wait_ge(sem("mod_done"), l + 1)
                for k in range(KT):
                    i = tr(B(4 + 2 * slot + k // 4)[:, (k % 4) * P:(k % 4 + 1) * P],
                           xh[:, slot, k * P:(k + 1) * P])
                i.then_inc(sem("n_tp"), 1)

            pe.wait_ge(sem("sc_ready"), 1)
            pe.wait_ge(sem("const_in"), 48)
            for n in range(6):
                mod_chunk(0, n, n % 2, n // 2)
            mod_turn(0)
            nine(pe, None, lambda t, slot, turn: norm(0, t, slot))
            pe.wait_ge(sem("n_ev"), NT)

            def project(c, slot, sname, wait):
                for n in range(3):
                    wait(n)
                    for k in range(KT):
                        i = mm(B(slot * 3 + n)[:, 0:NC], w0[:, slot, k], HT[:, k, n * NC:(n + 1) * NC],
                               start=(k == 0), stop=(k == KT - 1))
                    i.then_inc(sem(sname), 1)

            for c in range(4):
                pe.wait_ge(sem(f"w0_in{c % 2}"), 16 * (c // 2 + 1))
                project(c, c % 2, "xa_mm",
                        lambda n: pe.wait_ge(sem("xa_ev"), 3 * c + n - 5) if c >= 2 else None)

            def gates(m):
                first = isinstance(m, int) and m == 0
                for q in range(2):
                    pe.wait_ge(sem(f"w0_in{q}"), 16 * m + 48)
                    project(m, q, "g_mm",
                            lambda n: pe.wait_ge(sem("xa_ev"), 6 + 3 * q + n + 1) if first
                            else pe.wait_ge(sem("g_ev"), 6 * m + 3 * q + n - 5))
                pe.wait_ge(sem("gw_in"), 16 * m + 16)
                pe.wait_ge(sem("xc_ready"), m + 1)
                for i in range(6):
                    if not first or i >= 2:
                        pe.wait_ge(sem("lz_ev"), 6 * m + i - 1)
                    mm(B(6 + i % 2)[:, 0:NC], gw[:, i // 3], xc[:, (i % 3) * NC:(i % 3 + 1) * NC],
                       start=True, stop=True).then_inc(sem("l_mm"), 1)

            tiles(pe, None, LM, gates)
            pe.wait_ge(sem("g_ev"), 6 * LM)
            pe.wait_ge(sem("lz_ev"), 6 * LM)
            pe.wait_ge(sem("wqkv_in"), 16)

            def kv(t):
                pe.wait_ge(sem("hst_ready"), t + 1)
                if not (isinstance(t, int) and t == 0):
                    pe.wait_ge(sem("qkv_ev"), t)
                for k in range(KT):
                    mm(B(1)[:, 0:256], hst[:, k], wqkv[:, k, 512:], start=(k == 0), stop=(k == KT - 1))

            def queries(t):
                for k in range(KT):
                    i = mm(B(0), hst[:, k], wqkv[:, k, 0:512], start=(k == 0), stop=(k == KT - 1))
                i.then_inc(sem("qkv_mm"), 1)

            def att(t):
                first = isinstance(t, int) and t == 0
                sample = isinstance(t, int) and t == NT - 1
                pe.wait_ge(sem("rope_done"), t + 1)
                if not first:
                    pe.wait_ge(sem("qT_ev"), t)
                    pe.wait_ge(sem("o_ev"), t)
                for j in range(4):
                    tr(B(2)[:, j * P:(j + 1) * P], QK[:, 2 * j:2 * j + 2].rearrange("p v d -> p (v d)"))
                tr(B(3)[:, 0:P], QK[:, 8:10].rearrange("p v d -> p (v d)")).then_inc(sem("qk_tp"), 1)
                if not sample:
                    kv(t + 1)
                pe.wait_ge(sem("qT_ev"), t + 1)
                if not sample:
                    pe.wait_ge(sem("kw_ready"), t + 1)
                for u in range(4):
                    if not first or u >= 2:
                        pe.wait_ge(sem("s_add"), 4 * t + u - 1)
                    for a in range(2):
                        if sample:
                            s = 2 * u + a
                            for v in range(2):
                                vs = slice(v * HD, (v + 1) * HD)
                                q = qT.rearrange("p j t -> p (j t)")[vs, s * 64:(s + 1) * 64]
                                mm(B(4 + u % 2)[vs, a * 256:a * 256 + P], q, kc[vs, s],
                                   start=True, stop=True)
                                i = mm(B(4 + u % 2)[vs, a * 256 + P:a * 256 + 256], q,
                                       kT[vs, NT * P:(NT + 1) * P], start=True, stop=True)
                        else:
                            v, j = u // 2, 2 * (u % 2) + a
                            vs = slice(v * HD, (v + 1) * HD)
                            i = mm(B(4 + u % 2)[:, a * 256:(a + 1) * 256], qT[vs, j],
                                   kw[vs], start=True, stop=True)
                    i.then_inc(sem("s_mm"), 1)
                if not sample:
                    queries(t + 1)
                    pe.wait_ge(sem("vw_ready"), t + 1)

                def turn(u):
                    pe.wait_ge(sem("p_norm"), 4 * t + u + 1)
                    if not first or u >= 2:
                        pe.wait_ge(sem("pt_ev"), 4 * t + u - 1)
                    for a in range(2):
                        for w in range(2):
                            i = tr(B(6 + u % 2)[:, (2 * a + w) * P:(2 * a + w + 1) * P],
                                   SS[:, 2 * u + a, w * P:(w + 1) * P])
                    i.then_inc(sem("pt_tp"), 1)

                def weigh(u):
                    pe.wait_ge(sem("pt_ev"), 4 * t + u + 1)
                    for a in range(2):
                        if sample:
                            s = 2 * u + a
                            for v in range(2):
                                vs = slice(v * HD, (v + 1) * HD)
                                o = B(3)[vs, s * HD:(s + 1) * HD]
                                mm(o, vc[:, s, vs], PT[:, u % 2, 2 * a, vs], start=True, stop=False)
                                i = mm(o, V[:, NT, vs], PT[:, u % 2, 2 * a + 1, vs],
                                       start=False, stop=True)
                        else:
                            v, j = u // 2, 2 * (u % 2) + a
                            o = B(3)[v * HD:(v + 1) * HD, j * P:(j + 1) * P]
                            for w in range(2):
                                i = mm(o, vw[:, w, v * HD:(v + 1) * HD], PT[:, u % 2, 2 * a + w],
                                       start=(w == 0), stop=(w == 1))
                    i.then_inc(sem("pv_mm"), 1)

                turn(0)
                for u in range(1, 4):
                    turn(u)
                    weigh(u - 1)
                weigh(3)

            kv(0)
            queries(0)
            tiles(pe, None, 7, att)
            att(7)
            att(8)
            pe.wait_ge(sem("o_ev"), NT)
            pe.wait_ge(sem("wout_in"), 32)

            def out(l, t, slot, st, w):
                T = l * NT + t
                pe.wait_ge(sem("yst_ready"), T + 1)
                if past(T, 2):
                    pe.wait_ge(sem("out_ev"), T - 1)
                for n in range(2):
                    for k in range(KT):
                        i = mm(B(2 * slot + n), st[:, slot, k], w[:, k, n * 512:(n + 1) * 512],
                               start=(k == 0), stop=(k == KT - 1))
                i.then_inc(sem("out_mm"), 1)

            def out0(t, slot, turn):
                out(0, t, slot, yst, wout)
                if not (isinstance(t, int) and t in (0, 7, 8)):
                    mod_chunk(1, t - 1, 1 - slot, turn + slot - 1)

            nine(pe, None, out0)
            pe.wait_ge(sem("out_ev"), NT)
            mod_turn(1)
            nine(pe, None, lambda t, slot, turn: norm(1, t, slot))
            pe.wait_ge(sem("n_ev"), 2 * NT)

            pe.wait_ge(sem("ba_in"), 64)
            for n in range(3):
                for k in range(KT):
                    i = mm(B(5 + n)[0:40, 0:NC], wba[:, k], HT[:, k, n * NC:(n + 1) * NC],
                           start=(k == 0), stop=(k == KT - 1))
            i.then_inc(sem("ba_mm"), 1)

            def product(h, j):
                g, k = divmod(j, KT)
                m, n = divmod(g, 3)
                if k == 0:
                    if n == 0:
                        pe.wait_ge(sem(f"w1_in{m}"), 16 * h + 16)
                    if g < 2:
                        if not (isinstance(h, int) and h == 0):
                            pe.wait_ge(sem("z_ev"), 3 * h + g - 1)
                    elif g < 11:
                        pe.wait_ge(sem("pj_ev"), 9 * h + g - 1)
                    else:
                        pe.wait_ge(sem("z_ev"), 3 * h + 1)
                i = mm(B(g % 2)[:, 0:NC], wr[:, m, k], HT[:, k, n * NC:(n + 1) * NC],
                       start=(k == 0), stop=(k == KT - 1))
                if k == KT - 1:
                    i.then_inc(sem("pj_mm"), 1)

            def delta(h, b, ahead):
                first = isinstance(h, int) and h == 0 and b == 0
                nb = 4 if b < 2 else 1
                T = 3 * h + b
                col = lambda m, i: S1[:, m, (4 * b + i) * P:(4 * b + i + 1) * P]
                at_ = lambda bk, i: B(bk)[:, i * P:(i + 1) * P]
                place = iter(range(len(PLACES[b])))

                def between():
                    for j in range(*PLACES[b][next(place)]):
                        if ahead:
                            product(h + 1, j)

                pe.wait_ge(sem("s1_ready"), 3 * h + 3)
                if not first:
                    pe.wait_ge(sem("y1_done"), T)
                for m, bk, name in ((1, 2, "tk"), (0, 3, "tq"), (2, 4, "tv")):
                    for i in range(nb):
                        x = tr(at_(bk, i), col(m, i))
                    x.then_inc(sem(name), 1)
                between()
                pe.wait_ge(sem("kn_ready"), T + 1)
                for i in range(nb):
                    x = tr(at_(5, i), KN[:, i])
                x.then_inc(sem("tkn"), 1)
                between()
                pe.wait_ge(sem("knt_ready"), T + 1)
                pe.wait_ge(sem("ssq"), T + 1)
                for i in range(nb):
                    mm(at_(2, i), knt(b, i), knt(b, i), start=True, stop=True)
                    x = mm(at_(3, i), knt(b, i), col(0, i), start=True, stop=True)
                x.then_inc(sem("gq_mm"), 1)
                W0, L0, X0 = 15 * h + 6 * b, 18 * h + 7 * b, 16 * h + 6 * b
                between()
                pe.wait_ge(sem("vb_ready"), T + 1)
                pe.wait_ge(sem("y0_ready"), T + 1)
                for i in range(nb):
                    x = tr(at_(4, i), YI[:, i])
                x.then_inc(sem("x_tp"), 1)
                levels = 6 if b < 2 else 3
                for lv in range(1, levels + 1):
                    pe.wait_ge(sem("lv1_ready" if lv == 1 else "lv_ready"), T + 1 if lv == 1 else L0 + lv + 1)
                    pe.wait_ge(sem("xi_ready" if lv == 1 else "n_ev1"), T + 1 if lv == 1 else W0 + lv - 1)
                    for i in range(nb):
                        x = mm(at_(5, i), LV[:, lv % 2, i], XI[:, i], start=True, stop=True)
                    x.then_inc(sem("w_mm"), 1)
                    between()
                    pe.wait_ge(sem("w_ev"), W0 + lv)
                    if lv == 1:
                        pe.wait_ge(sem("um_ready"), T + 1)
                    if lv > 1:
                        pe.wait_ge(sem("y_ev"), 13 * h + 5 * b + lv - 1)
                    for i in range(nb):
                        if lv < 6:
                            x = mm(at_(2, i), YI[:, i], WI[:, i], start=True, stop=True)
                        else:
                            x = mm(at_(2, i), WI[:, i], YI[:, i], start=True, stop=True)
                    x.then_inc(sem("n_mm"), 1)
                    between()
                    pe.wait_ge(sem("n_ev1"), W0 + lv)
                    if lv < 6:
                        for i in range(nb):
                            x = tr(at_(4, i), XI[:, i])
                        x.then_inc(sem("x_tp"), 1)
                        between()
                if b == 2:
                    pe.wait_ge(sem("y_ev"), 13 * h + 13)
                pe.wait_ge(sem("kd_ready"), T + 1)
                pe.wait_ge(sem("qkt_ready"), T + 1)
                for i in range(nb):
                    c = 9 * h + 4 * b + i
                    if b < 2:
                        pe.wait_ge(sem("st_ready"), c + 1)
                        mm(at_(6, 0), knt(b, i), SP, start=True, stop=True).then_inc(sem("ks_mm"), 1)
                        if not (first and i == 0):
                            pe.wait_ge(sem("o_ready"), c)
                        mm(at_(7, 0), col(0, i), SP, start=True, stop=True).then_inc(sem("qs_mm"), 1)
                    else:
                        pe.wait_ge(sem("ss_in"), 16 * h + 16)
                        pe.wait_ge(sem("kq_ready"), h + 1)
                        pe.wait_ge(sem("st_ready"), c + 1)
                        pe.wait_ge(sem("o_ready"), c)
                        for s_ in range(NS):
                            x = mm(B(6)[:, s_ * 32:(s_ + 1) * 32], SS1[:, s_],
                                   KQ[:, :, s_ * DS:(s_ + 1) * DS], start=True, stop=True)
                        x.then_inc(sem("kqs_mm"), 1)
                        between()
                        pe.wait_ge(sem("kqs_ev"), h + 1)
                        tr(at_(6, 0), KQS[:, 0]).then_inc(sem("ks_mm"), 1)
                        tr(at_(7, 0), KQS[:, 1]).then_inc(sem("qs_mm"), 1)
                    between()
                    pe.wait_ge(sem("r_ready"), c + 1)
                    mm(at_(6, 1), YI[:, i], RR, start=True, stop=True).then_inc(sem("tr_mm"), 1)
                    between()
                    pe.wait_ge(sem("vn_ready"), c + 1)
                    if b < 2:
                        mm(at_(6, 2), KD[:, i], VN, start=True, stop=True).then_inc(sem("kv_mm"), 1)
                    pe.wait_ge(sem("qe_ready"), c + 1)
                    mm(at_(7, 1), EQ[:, i], VN, start=True, stop=True).then_inc(sem("o_mm"), 1)
                    if b == 2:
                        pe.wait_ge(sem("vm_ready"), h + 1)
                        for g in range(2):
                            x = mm(B(4 + g), KD[:, 0], VM[:, 4 * g:4 * g + 4].rearrange("p s v -> p (s v)"),
                                   start=True, stop=True)
                        x.then_inc(sem("skv_mm"), 1)
                    between()
                between()
                pe.wait_ge(sem("on_ready"), T + 1)
                for i in range(nb):
                    x = tr(at_(2, i), ON[:, i])
                x.then_inc(sem("o_tp"), 1)
                between()
                assert not list(place)

            def head(h, ahead=True):
                for b in range(3):
                    delta(h, b, ahead)

            for j in range(BA_GROUPS * KT):
                product(0, j)
            pe.wait_ge(sem("rows_ready"), 1)
            for q in range(3):
                for t in range(NT):
                    i = tr(B(3)[:, (q * NT + t) * H:(q * NT + t + 1) * H],
                           GR[0:H, q, t * P:(t + 1) * P], H)
            i.then_inc(sem("col_tr"), 1)
            for j in range(BA_GROUPS * KT, GROUPS * KT):
                product(0, j)
            tiles(pe, None, H - 1, head)
            head(H - 1, False)
            pe.wait_ge(sem("y1_done"), 3 * H)
            pe.wait_ge(sem("z_ev"), 3 * H)
            pe.wait_ge(sem("wout1_in"), 16)
            nine(pe, None, lambda t, slot, turn: out(1, t, slot, yst1, wout1))

        @block.scalar
        def _(act):
            c = Count(act, sem("act_own"))
            PASSED[act.engine] = sem("act_passed")
            wait(act, sem("const_in"), 48)
            act.activation(ctmp, cT, ACT.Tanh, scale=0.5).then_inc(sem("c_th"), 1)

            def square(l, t, slot):
                if l or past(t, 1):
                    wait(act, sem("n_ss"), l * NT + t)
                act.activation(oj, X[:, bass.ds(t, 1)].rearrange("p a d -> p (a d)"), ACT.Square,
                               accum_out=stat[:, 3 * slot:3 * slot + 1]).then_inc(sem("n_ss"), 1)

            def norm(l, t, slot):
                if not (isinstance(t, int) and t == NT - 1):
                    square(l, t + 1, 1 - slot)
                wait(act, sem("n_rs"), l * NT + t + 1)
                if l or past(t, 2):
                    wait(act, sem("n_tp"), l * NT + t - 1)
                act.activation(xh[:, slot], X[:, bass.ds(t, 1)].rearrange("p a d -> p (a d)"), ACT.Copy,
                               scale=stat[:, 3 * slot + 2:3 * slot + 3]).then_inc(sem("n_xh"), 1)

            wait(act, sem("x_in"), 16)
            square(0, 0, 0)
            nine(act, None, lambda t, slot, turn: norm(0, t, slot))
            wait(act, sem("lru_in"), 16 * 8)
            c.mark(act.activation(ltmp[:, 0], lam, ACT.Abs))
            c.sync()
            c.mark(act.activation(ltmp[:, 1], ltmp[:, 0], ACT.Exp, scale=-1.0))
            c.sync()
            act.activation(ltmp[:, 2], ltmp[:, 1], ACT.Ln, bias=1.0).then_inc(sem("sp_ln"), 1)
            for m in range(4):
                for n in range(3):
                    wait(act, sem("xa_mm"), 3 * m + n + 1)
                    b = B((m % 2) * 3 + n)
                    if n < 2:
                        i = act.activation(UA[:, m, PRE + n * NC:PRE + (n + 1) * NC], b[:, 0:NC], ACT.Copy)
                    else:
                        r = SEQ - 2 * NC
                        c.mark(act.activation(UA[:, m, PRE + 2 * NC:PRE + SEQ], b[:, 0:r], ACT.Copy))
                        i = act.activation(
                            UA[:, m, US:].rearrange("p (s u) -> p s u", s=NS)[:, :, PRE:],
                            b[:, r:NC].rearrange("p (s u) -> p s u", s=NS), ACT.Copy)
                    i.then_inc(sem("xa_ev"), 1)

            def lru(m):
                first = isinstance(m, int) and m == 0
                if first:
                    wait(act, sem("l_const"), 1)
                for g in range(6):
                    wait(act, sem("g_mm"), 6 * m + g + 1)
                    if not first or g >= 2:
                        wait(act, sem("g_ev"), 6 * m + g - 1)
                    act.activation(th[:, g % 2], B(g)[:, 0:NC], ACT.Tanh, scale=0.5
                                   ).then_inc(sem("g_th"), 1)
                for i in range(6):
                    wait(act, sem("l_mm"), 6 * m + i + 1)
                    if not first and i == 0:
                        wait(act, sem("l_y"), m)
                    dst = (tr, ti)[i // 3][:, (i % 3) * NC:(i % 3 + 1) * NC]
                    act.activation(dst, B(6 + i % 2)[:, 0:NC], ACT.Tanh, scale=0.5,
                                   bias=gbias[:, bass.ds(m, 1), i // 3]).then_inc(sem("lz_ev"), 1)
                wait(act, sem("lz_ev"), 6 * m + 3)
                c.mark(act.activation(la, tr, ACT.Exp, scale=ksp[:, bass.ds(m, 1)],
                                      bias=ksp[:, bass.ds(m, 1)]))
                act.activation(lw_, tr, ACT.Tanh, scale=kneg[:, bass.ds(m, 1)],
                               bias=kneg[:, bass.ds(m, 1)]).then_inc(sem("l_a"), 1)
                wait(act, sem("l_w"), m + 1)
                act.activation(lw_, lw_, ACT.Sqrt).then_inc(sem("l_sq"), 1)

            tiles(act, c, LM, lru)

            def qkv_ev(t):
                wait(act, sem("qkv_mm"), t + 1)
                if not (isinstance(t, int) and t == 0):
                    wait(act, sem("qk_tp"), t)
                if isinstance(t, int) and t == 0:
                    wait(act, sem("l_y"), LM)
                    wait(act, sem("out0"), 32)
                if isinstance(t, int) and t == 8:
                    wait(act, sem("kout"), 16)
                c.mark(act.activation(QK[:, 0:8].rearrange("p (j v) d -> p v j d", v=2),
                                      B(0).rearrange("p (v j d) -> p v j d", v=2, j=4), ACT.Copy))
                c.mark(act.activation(QK[:, 8:10].rearrange("p v d -> p (v d)"), B(1)[:, 0:P], ACT.Copy))
                act.activation(V[:, bass.ds(t + 1, 1)].rearrange("p a d -> p (a d)"), B(1)[:, P:2 * P],
                               ACT.Copy).then_inc(sem("qkv_ev"), 1)

            def att(t):
                first = isinstance(t, int) and t == 0
                wait(act, sem("qk_tp"), t + 1)
                if not first:
                    wait(act, sem("s_mm"), 4 * t)
                if isinstance(t, int) and t == NT - 1:
                    c.mark(act.activation(
                        qT.rearrange("p j t -> p (j t)").rearrange("p (s j u) -> p j s u", s=NS, j=4),
                        B(2).rearrange("p (j s u) -> p j s u", s=NS, j=4), ACT.Copy))
                else:
                    c.mark(act.activation(qT.rearrange("p j t -> p (j t)"), B(2), ACT.Copy))
                act.activation(kT[:, bass.ds(t * P + P, P)], B(3)[:, 0:P], ACT.Copy
                               ).then_inc(sem("qT_ev"), 1)
                wait(act, sem("s_stat"), t + 1)
                for a in range(8):
                    c.mark(act.activation(SS[:, a], SS[:, a], ACT.Exp, scale=HD ** -0.5,
                                          bias=nm[:, a:a + 1], accum_out=den[:, a:a + 1]))
                act.activation(es, es, ACT.Exp).then_inc(sem("p_exp"), 1)
                if not (isinstance(t, int) and t == 8):
                    qkv_ev(t + 1)
                for u in range(4):
                    wait(act, sem("pt_tp"), 4 * t + u + 1)
                    if not first or u >= 2:
                        wait(act, sem("pv_mm"), 4 * t + u - 1)
                    act.activation(PT[:, u % 2].rearrange("p a t -> p (a t)"), B(6 + u % 2), ACT.Copy
                                   ).then_inc(sem("pt_ev"), 1)

            qkv_ev(0)
            tiles(act, c, 7, att)
            att(7)
            att(8)

            def out(l, t, slot, junk):
                T = l * NT + t
                for n in range(2):
                    if n == 0:
                        wait(act, sem("out_mm"), T + 1)
                        if past(T, 1):
                            wait(act, sem("o_ss"), T)
                    st = 6 + 5 * slot + n
                    i = act.activation(junk[:, n * 512:(n + 1) * 512], B(2 * slot + n), ACT.Square,
                                       accum_out=stat[:, st:st + 1])
                    if n == 0:
                        c.mark(i)
                i.then_inc(sem("o_ss"), 1)

            nine(act, c, lambda t, slot, turn: out(0, t, slot, oj))
            wait(act, sem("x1_done"), NT)
            wait(act, sem("o_ss"), NT)
            square(1, 0, 0)
            nine(act, None, lambda t, slot, turn: norm(1, t, slot))

            act.wait_ge(sem("ba_mm"), 1)
            act.wait_ge(sem("n_tp"), 2 * NT)
            for n in range(3):
                c.mark(act.activation(Z[0:H, 0, n * NC:(n + 1) * NC], B(5 + n)[0:H, 0:NC], ACT.Copy, scale=-1.0))
                c.mark(act.activation(Z[0:H, 1, n * NC:(n + 1) * NC], B(5 + n)[32:40, 0:NC], ACT.Copy))
            c.sync()
            c.mark(act.activation(Z[0:H, 1], Z[0:H, 1], ACT.Identity, bias=dtb[0:H]))
            c.sync()
            c.mark(act.activation(Z1[0:H], Z[0:H], ACT.Abs))
            c.sync()
            c.mark(act.activation(Z1[0:H], Z1[0:H], ACT.Exp, scale=-1.0))
            c.mark(act.activation(nega[0:H], nega[0:H], ACT.Exp))
            c.sync()
            act.activation(Z1[0:H], Z1[0:H], ACT.Ln, bias=1.0).then_inc(sem("ba_ln"), 1)

            act.wait_ge(sem("x1_out"), 16)

            def leave(h, g):
                first = isinstance(h, int) and h == 0
                m, n = divmod(g, 3)
                bk = B(g % 2)
                wait(act, sem("pj_mm"), 12 * h + g + 1)
                if m == 3:
                    if not first or n >= 2:
                        wait(act, sem("z_ev"), 3 * h + n - 1)
                    act.activation(zt[:, n % 2], bk[:, 0:NC], ACT.Tanh, scale=0.5
                                   ).then_inc(sem("z_th"), 1)
                    return
                if not first and n == 0:
                    wait(act, sem("cv_done"), 3 * h)
                    wait(act, sem("hist1"), 6 * h)
                if n < 2:
                    i = act.activation(U1[:, m, PRE + n * NC:PRE + (n + 1) * NC], bk[:, 0:NC], ACT.Copy)
                else:
                    r = SEQ - 2 * NC
                    c.mark(act.activation(U1[:, m, PRE + 2 * NC:US], bk[:, 0:r], ACT.Copy))
                    i = act.activation(
                        U1[:, m, US:].rearrange("p (s u) -> p s u", s=NS)[:, :, PRE:],
                        bk[:, r:NC].rearrange("p (s u) -> p s u", s=NS), ACT.Copy)
                i.then_inc(sem("pj_ev"), 1)

            def silu_tanh(h, m):
                wait(act, sem("cv_done"), 3 * h + m + 1)
                if not (isinstance(h, int) and h == 0 and m == 0):
                    wait(act, sem("s1_ready"), 3 * h + m)
                act.activation(TH1[:, 0:UC], CV[:, m, 0:UC], ACT.Tanh, scale=0.5
                               ).then_inc(sem("th1"), 1)

            def delta(h, b, ahead):
                nb = 4 if b < 2 else 1
                T = 3 * h + b
                W0 = 15 * h + 6 * b
                place = iter(range(len(PLACES[b])))

                def between():
                    p = next(place)
                    if ahead:
                        for g in ended(b, p):
                            leave(h + 1, g)
                        if b == 2 and p in (3, 6, 9):
                            silu_tanh(h + 1, p // 3 - 1)

                wait(act, sem("tk"), T + 1)
                for i in range(nb):
                    if i:
                        c.sync()
                    x = act.activation(SQJ, B(2)[:, i * P:(i + 1) * P], ACT.Square,
                                       accum_out=ssk[:, i:i + 1])
                    if i < nb - 1:
                        c.mark(x)
                c.tell(x, sem("ssk"), T + 1)
                wait(act, sem("e_arg"), T + 1)
                c.mark(act.activation(EA[:, 0:nb], EA[:, 0:nb], ACT.Exp))
                act.activation(EQ[:, 0:nb], EQ[:, 0:nb], ACT.Exp).then_inc(sem("e_exp"), 1)
                wait(act, sem("tq"), T + 1)
                wait(act, sem("ssk"), T + 1)
                for i in range(nb):
                    if i:
                        c.sync()
                    x = act.activation(SQJ, B(3)[:, i * P:(i + 1) * P], ACT.Square,
                                       accum_out=ssq[:, i:i + 1])
                    if i < nb - 1:
                        c.mark(x)
                c.tell(x, sem("ssq"), T + 1)
                between()
                wait(act, sem("tkn"), T + 1)
                dst = KNT[:, 0:nb].rearrange("p a t -> p (a t)") if b < 2 else KQ[:, 0]
                act.activation(dst, B(5)[:, 0:nb * P], ACT.Copy).then_inc(sem("knt_ready"), 1)
                between()
                between()
                flat = lambda a: a[:, 0:nb].rearrange("p a t -> p (a t)")
                wait(act, sem("x_tp"), 16 * h + 6 * b + 1)
                act.activation(flat(XI), B(4)[:, 0:nb * P], ACT.Copy).then_inc(sem("xi_ready"), 1)
                for lv in range(1, (6 if b < 2 else 3) + 1):
                    wait(act, sem("w_mm"), W0 + lv)
                    act.activation(flat(WI), B(5)[:, 0:nb * P], ACT.Copy).then_inc(sem("w_ev"), 1)
                    between()
                    between()
                    if lv < 6:
                        wait(act, sem("x_tp"), 16 * h + 6 * b + 1 + lv)
                        act.activation(flat(YI), B(4)[:, 0:nb * P], ACT.Copy).then_inc(sem("y_ev"), 1)
                        between()
                for i in range(nb):
                    cc = 9 * h + 4 * b + i
                    if b == 2:
                        between()
                    wait(act, sem("qs_mm"), cc + 1)
                    if not (isinstance(h, int) and h == 0 and b == 0 and i == 0):
                        wait(act, sem("o_ready"), cc)
                    act.activation(QE, B(7)[:, 0:P], ACT.Copy, scale=HC[:, 1, 4 * b + i:4 * b + i + 1]
                                   ).then_inc(sem("qe_ready"), 1)
                    between()
                    between()
                    wait(act, sem("o_ready"), cc + 1)
                    if i == 0:
                        wait(act, sem("ssq"), T + 1)
                    else:
                        c.sync()
                    x = act.activation(SQJ, OO[:, i], ACT.Square, accum_out=sso[:, i:i + 1])
                    if i < nb - 1:
                        c.mark(x)
                    else:
                        c.tell(x, sem("sso"), T + 1)
                    between()
                between()
                between()
                assert not list(place)

            def head(h, ahead=True):
                for b in range(3):
                    if b == 0:
                        if not (isinstance(h, int) and h == 0):
                            wait(act, sem("sso"), 3 * h)
                    else:
                        wait(act, sem("sso"), 3 * h + b)
                    delta(h, b, ahead)

            for g in range(BA_GROUPS):
                leave(0, g)
            act.wait_ge(sem("gl_ready"), 1)
            act.activation(GL[0:H], GL[0:H], ACT.Exp).then_inc(sem("rows_ready"), 1)
            act.wait_ge(sem("ca_arg"), 1)
            act.activation(CA[:, 1:], CA[:, 1:], ACT.Exp).then_inc(sem("ca_exp"), 1)
            act.wait_ge(sem("rows_out"), 48)
            for g in range(BA_GROUPS, GROUPS):
                leave(0, g)
            for m in range(3):
                silu_tanh(0, m)
            tiles(act, c, H - 1, head)
            head(H - 1, False)
            wait(act, sem("pj_mm"), GROUPS * H)
            nine(act, c, lambda t, slot, turn: out(1, t, slot, oj1))

        @block.vector
        def _(dve):
            c = Count(dve, sem("dve_own"))
            PASSED[dve.engine] = sem("dve_passed")
            dve.wait_ge(sem("c_th"), 1)
            c.mark(dve.scalar_tensor_tensor(ctmp, ctmp, 1.0, cT, ALU.add, ALU.mult))
            c.sync()
            dve.tensor_scalar(scT, ctmp, 0.5, None, ALU.mult).then_inc(sem("sc_ready"), 1)

            def mod_chunk(l, n, slot):
                dve.wait_ge(sem("mod_mm"), 6 * l + 1 + n)
                r = bass.ds(n * 512, 512)
                dve.tensor_tensor(modrow[0:9, r], B(4 + slot)[0:9], modb[0:9, r], ALU.add
                                  ).then_inc(sem("mod_ev"), 1)

            def mod(l):
                dve.wait_ge(sem("mod_ev"), 6 * l + 6)
                dve.tensor_tensor(modrow[0:9, 2 * D:], modrow[0:9, 2 * D:], npost[0:9], ALU.mult
                                  ).then_inc(sem("mod_row"), 1)
                dve.wait_ge(sem("mod_tr"), l + 1)
                c.mark(dve.tensor_copy(modT.rearrange("p a b -> p (a b)"), B(6)[:, 0:144]))
                c.sync()
                c.mark(dve.tensor_scalar(modT[:, KT:], modT[:, KT:], 1.0, None, ALU.add))
                c.sync()
                c.mark(dve.tensor_tensor(modT[:, KT:], modT[:, KT:], bc(npre[:, l], 2, 9), ALU.mult))
                c.mark(dve.tensor_copy(gate[:, 0], psum[:, 0:2].rearrange("p a b -> p (a b)")))
                dve.tensor_copy(gate[:, 1], psum[:, 2:4].rearrange("p a b -> p (a b)")
                                ).then_inc(sem("mod_done"), 1)
                dve.wait_ge(sem("mod_done"), l + 1)

            def norm(l, t, slot):
                sample = isinstance(t, int) and t == NT - 1
                dve.wait_ge(sem("n_tp"), l * NT + t + 1)
                src = [B(4 + 2 * slot + k // 4)[:, (k % 4) * P:(k % 4 + 1) * P] for k in range(KT)]
                if not sample:
                    for k in range(KT):
                        i = dve.tensor_scalar(HT[:, k, bass.ds(t * P, P)], src[k],
                                              modT[:, KT + k, 0:1], modT[:, k, 0:1], ALU.mult, ALU.add)
                        if k < KT - 1:
                            c.mark(i)
                else:
                    sq = lambda a: a.rearrange("p (s u) -> p s u", s=NS)
                    for k in range(KT):
                        c.mark(dve.tensor_tensor(sq(HT[:, k, SEQ:]), sq(src[k]),
                                                 bc(modT[:, KT + k, 1:], 2, DS), ALU.mult))
                    c.sync()
                    for k in range(KT):
                        i = dve.tensor_tensor(sq(HT[:, k, SEQ:]), sq(HT[:, k, SEQ:]),
                                              bc(modT[:, k, 1:], 2, DS), ALU.add)
                i.then_inc(sem("n_ev"), 1)

            dve.wait_ge(sem("modb_in"), 48)
            for n in range(6):
                mod_chunk(0, n, n % 2)
            mod(0)
            nine(dve, c, lambda t, slot, turn: norm(0, t, slot))

            dve.wait_ge(sem("sp_ln"), 1)
            c.mark(dve.tensor_scalar(ltmp[:, 3], lam, -1.0, 0.0, ALU.mult, ALU.max))
            c.mark(dve.tensor_scalar(gbias, gbias, 0.5, None, ALU.mult))
            c.sync()
            c.mark(dve.tensor_tensor(ltmp[:, 3], ltmp[:, 3], ltmp[:, 2], ALU.add))
            c.sync()
            c.mark(dve.tensor_scalar(kneg, ltmp[:, 3], 4.0, None, ALU.mult))
            dve.tensor_scalar(ksp, ltmp[:, 3], -4.0, None, ALU.mult).then_inc(sem("l_const"), 1)
            dve.wait_ge(sem("ua_zero"), 1)

            def lru(m):
                first = isinstance(m, int) and m == 0
                one = bass.ds(m, 1)
                if first:
                    dve.wait_ge(sem("xa_ev"), 12)
                else:
                    dve.wait_ge(sem("l_y"), m)
                c.sync()
                u = lambda j: UA[:, one, j:j + UC].rearrange("p a u -> p (a u)")
                w = lambda j: cw0[:, one, j]
                c.mark(dve.tensor_scalar(cv, u(0), w(0), w(TAPS), ALU.mult, ALU.add))
                c.sync()
                for j in (1, 2):
                    c.mark(dve.scalar_tensor_tensor(cv, u(j), w(j), cv, ALU.mult, ALU.add))
                    c.sync()
                c.mark(dve.scalar_tensor_tensor(xc[:, 0:SEQ], u(3)[:, 0:SEQ], w(3), cv[:, 0:SEQ],
                                                ALU.mult, ALU.add))
                us = UA[:, one, US:].rearrange("p a (s u) -> p (a s) u", s=NS)[:, :, PRE:]
                cs = cv_row[:, US:].rearrange("p (s u) -> p s u", s=NS)[:, :, 0:DS]
                dve.scalar_tensor_tensor(xc[:, SEQ:].rearrange("p (s u) -> p s u", s=NS), us, w(3), cs,
                                         ALU.mult, ALU.add).then_inc(sem("xc_ready"), 1)
                for g in range(6):
                    dve.wait_ge(sem("g_th"), 6 * m + g + 1)
                    row = m if g < 3 else m + 4
                    dst = YT[:, bass.ds(row, 1), (g % 3) * NC:(g % 3 + 1) * NC].rearrange("p a t -> p (a t)")
                    dve.scalar_tensor_tensor(dst, th[:, g % 2], 1.0, B(g)[:, 0:NC], ALU.add, ALU.mult
                                             ).then_inc(sem("g_ev"), 1)
                dve.wait_ge(sem("l_a"), m + 1)
                dve.wait_ge(sem("lz_ev"), 6 * m + 6)
                c.mark(dve.tensor_tensor(lg, la, la, ALU.mult))
                c.sync()
                dve.scalar_tensor_tensor(lw_, lg, 1.0, lw_, ALU.add, ALU.mult).then_inc(sem("l_w"), 1)
                c.mark(dve.scalar_tensor_tensor(ti, ti, 1.0, xc, ALU.add, ALU.mult))
                dve.wait_ge(sem("l_sq"), m + 1)
                c.sync()
                c.mark(dve.scalar_tensor_tensor(lg, ti, 0.5, lw_, ALU.mult, ALU.mult))
                c.sync()
                c.mark(dve.tensor_tensor_scan(lh[:, 0:SEQ], la[:, 0:SEQ], lg[:, 0:SEQ], 0.0,
                                              ALU.mult, ALU.add))
                for s in range(NS):
                    r = slice(SEQ + s * DS, SEQ + (s + 1) * DS)
                    c.mark(dve.tensor_tensor_scan(lh[:, r], la[:, r], lg[:, r], h0[:, one, s],
                                                  ALU.mult, ALU.add))
                c.sync()
                c.mark(dve.tensor_copy(hc[:, one, 0], lh[:, SEQ - 1:SEQ]))
                c.mark(dve.tensor_copy(hc[:, one, 1:].rearrange("p a s -> p (a s)"),
                                       lh[:, SEQ + DS - 1:TOK:DS]))
                y = YT[:, one, :].rearrange("p a t -> p (a t)")
                dve.wait_ge(sem("g_ev"), 6 * m + 3)
                dve.scalar_tensor_tensor(y, lh, 0.5, y, ALU.mult, ALU.mult).then_inc(sem("l_y"), 1)

            tiles(dve, c, LM, lru)
            dve.wait_ge(sem("att_in"), 16 * 7)

            def rot(t):
                dve.wait_ge(sem("qkv_ev"), t + 1)
                cs = rope[:, bass.ds(t, 1), 0:16].rearrange("p a r -> p (a r)")
                sn = rope[:, bass.ds(t, 1), 16:32].rearrange("p a r -> p (a r)")
                c.mark(dve.tensor_tensor(ra, QK[:, :, 0:16], bc(cs, 1, 10), ALU.mult))
                c.mark(dve.tensor_tensor(rb[:, :, 0:8], QK[:, :, 8:16], bc(sn[:, 0:8], 1, 10), ALU.mult))
                c.mark(dve.tensor_tensor(rb[:, :, 8:16], QK[:, :, 0:8], bc(sn[:, 8:16], 1, 10), ALU.mult))
                c.sync()
                dve.tensor_tensor(QK[:, :, 0:16], ra, rb, ALU.add).then_inc(sem("rope_done"), 1)

            def att(t):
                first = isinstance(t, int) and t == 0
                sample = isinstance(t, int) and t == NT - 1
                for u in range(4):
                    dve.wait_ge(sem("s_mm"), 4 * t + u + 1)
                    if not first:
                        wait(dve, sem("pt_tp"), 4 * t + u - 3)
                    for a in range(2):
                        n = 2 * u + a
                        mask = smask[:, n] if sample else amask[:, 0 if first else 1]
                        i = dve.tensor_tensor_reduce(SS[:, n], B(4 + u % 2)[:, a * 256:(a + 1) * 256],
                                                     mask, 1.0, -3.0e38, ALU.add, ALU.max, mx[:, n:n + 1])
                        if a == 0:
                            c.mark(i)
                    i.then_inc(sem("s_add"), 1)
                sink = sinkS.broadcast_to([P, 8]) if sample else sinkP
                dve.wait_ge(sem("s_add"), 4 * t + 4)
                c.mark(dve.scalar_tensor_tensor(m2, mx, HD ** -0.5, sink, ALU.mult, ALU.max))
                c.sync()
                c.mark(dve.tensor_tensor(es, sink, m2, ALU.subtract))
                dve.tensor_scalar(nm, m2, -1.0, None, ALU.mult).then_inc(sem("s_stat"), 1)
                dve.wait_ge(sem("p_exp"), t + 1)
                c.mark(dve.tensor_tensor(d2, den, es, ALU.add))
                c.sync()
                c.mark(dve.reciprocal(rd, d2))
                c.sync()
                for u in range(4):
                    for a in range(2):
                        n = 2 * u + a
                        i = dve.tensor_scalar(SS[:, n], SS[:, n], rd[:, n:n + 1], None, ALU.mult)
                        if a == 0:
                            c.mark(i)
                    i.then_inc(sem("p_norm"), 1)
                if not sample:
                    rot(t + 1)
                dve.wait_ge(sem("pv_mm"), 4 * t + 4)
                if sample:
                    for j in range(4):
                        o = B(3).rearrange("p (s j u) -> p j s u", s=NS, j=4)[:, j]
                        y = YT[:, 4 + j, SEQ:].rearrange("p (s u) -> p s u", s=NS)
                        i = dve.scalar_tensor_tensor(y, o, 0.5, y, ALU.mult, ALU.mult)
                        if j < 3:
                            c.mark(i)
                    i.then_inc(sem("o_ev"), 1)
                else:
                    y = YT[:, 4:8, bass.ds(t * P, P)]
                    dve.scalar_tensor_tensor(y, B(3).rearrange("p (j u) -> p j u", j=4), 0.5, y,
                                             ALU.mult, ALU.mult).then_inc(sem("o_ev"), 1)

            rot(0)
            tiles(dve, c, 7, att)
            att(7)
            att(8)
            def out(l, t, slot, x, tmp):
                T = l * NT + t
                w = 1 if isinstance(t, int) and t == NT - 1 else 0
                if past(T, 1):
                    dve.wait_ge(sem("x1_done"), T)
                dve.wait_ge(sem("o_rs"), T + 1)
                rs = stat[:, 10 + 5 * slot:11 + 5 * slot]
                c.mark(dve.scalar_tensor_tensor(tmp[:, 0:512], B(2 * slot), rs, gate[:, w, 0:512],
                                                ALU.mult, ALU.mult))
                dve.scalar_tensor_tensor(tmp[:, 512:], B(2 * slot + 1), rs, gate[:, w, 512:],
                                         ALU.mult, ALU.mult).then_inc(sem("out_ev"), 1)
                dve.wait_ge(sem("out_ev"), T + 1)
                dve.tensor_tensor(x, x, tmp, ALU.add).then_inc(sem("x1_done"), 1)

            def out0(t, slot, turn):
                out(0, t, slot, X[:, bass.ds(t, 1)].rearrange("p a d -> p (a d)"), otmp)
                if not (isinstance(t, int) and t in (0, 7, 8)):
                    mod_chunk(1, t - 1, 1 - slot)

            dve.wait_ge(sem("modb_in"), 48 * 2)
            nine(dve, c, out0)
            dve.wait_ge(sem("x1_done"), NT)
            mod(1)
            nine(dve, c, lambda t, slot, turn: norm(1, t, slot))

            dve.wait_ge(sem("ba_ln"), 1)
            c.mark(dve.scalar_tensor_tensor(Z2[0:H], Z[0:H], 0.0, Z1[0:H], ALU.max, ALU.add))
            c.sync()
            c.mark(dve.tensor_scalar(Z[0:H, 1], Z2[0:H, 1], nega[0:H], -1.0, ALU.mult, ALU.mult))
            c.sync()
            c.mark(dve.tensor_tensor_scan(GR[0:H, 1], reset[0:H], Z[0:H, 1], 0.0, ALU.mult, ALU.add))
            c.sync()
            c.mark(dve.tensor_tensor(GR[0:H, 0], GR[0:H, 1], Z2[0:H, 0], ALU.subtract))
            c.mark(dve.tensor_copy(GL[0:H, 0:8], GR[0:H, 1, P - 1:SEQ:P]))
            c.mark(dve.tensor_copy(GL[0:H, 8:16], GR[0:H, 1, SEQ + DS - 1:TOK:DS]))
            c.sync()
            c.mark(dve.tensor_tensor(GR[0:H, 2, 0:SEQ].rearrange("p (c t) -> p c t", t=P),
                                     bc(GL[0:H, 0:8], 2, P),
                                     GR[0:H, 1, 0:SEQ].rearrange("p (c t) -> p c t", t=P), ALU.subtract))
            dve.tensor_tensor(GR[0:H, 2, SEQ:].rearrange("p (c t) -> p c t", t=DS),
                              bc(GL[0:H, 8:16], 2, DS),
                              GR[0:H, 1, SEQ:].rearrange("p (c t) -> p c t", t=DS), ALU.subtract
                              ).then_inc(sem("gl_ready"), 1)
            dve.wait_ge(sem("col_tr"), 1)
            tr3 = B(3)[:, 0:3 * NT * H].rearrange("p (q t h) -> p q t h", q=3, t=NT)
            c.mark(dve.tensor_copy(CA[:, 0], tr3[:, 1]))
            c.mark(dve.tensor_copy(CA[:, 1], tr3[:, 1]))
            c.mark(dve.tensor_copy(CA[:, 3], tr3[:, 0]))
            c.mark(dve.tensor_copy(CA[:, 4], tr3[:, 2]))
            c.sync()
            dve.tensor_tensor(CA[:, 2], CA[:, 3], CA[:, 0], ALU.subtract).then_inc(sem("ca_arg"), 1)
            dve.wait_ge(sem("ca_exp"), 1)
            c.mark(dve.tensor_scalar(CA[:, 2], CA[:, 2], 0.5, None, ALU.mult))
            c.mark(dve.tensor_scalar(CA[:, 3], CA[:, 3], -1.0, None, ALU.mult))
            dve.wait_ge(sem("l1_in"), 16 * 6)
            c.mark(dve.tensor_scalar(HN, HN, 0.5, None, ALU.mult))
            dve.wait_ge(sem("u1_zero"), 1)
            dve.wait_ge(sem("rows_out"), 48)
            c.sync()

            def conv(h, g, j):
                m, n = divmod(g, 3)
                lo, hi = n * NC, (n + 1) * NC if n < 2 else UC
                w = CW[:, bass.ds(h * 3 + m, 1), j]
                cvm = CV[:, m, lo:hi]
                if j == 0:
                    dve.wait_ge(sem("pj_ev"), 9 * h + g + 1)
                    if n == 2:
                        dve.wait_ge(sem("cs_in"), 48 * h + 48)
                    if n == 0 and not (isinstance(h, int) and h == 0):
                        dve.wait_ge(sem("s1_ready"), 3 * h)
                    c.mark(dve.tensor_scalar(cvm, U1[:, m, lo:hi], w, None, ALU.mult))
                else:
                    c.sync()
                    x = dve.scalar_tensor_tensor(cvm, U1[:, m, lo + j:hi + j], w, cvm, ALU.mult, ALU.add)
                    if n == 2 and j == PRE:
                        c.tell(x, sem("cv_done"), 3 * h + m + 1)
                    else:
                        c.mark(x)

            def gated(h, n):
                dve.wait_ge(sem("z_th"), 3 * h + n + 1)
                y = YT[:, bass.ds(h, 1), n * NC:(n + 1) * NC].rearrange("p a t -> p (a t)")
                dve.scalar_tensor_tensor(y, zt[:, n % 2], 1.0, B((9 + n) % 2)[:, 0:NC], ALU.add, ALU.mult
                                         ).then_inc(sem("z_ev"), 1)

            def silu(h, m):
                dve.wait_ge(sem("th1"), 3 * h + m + 1)
                if not (isinstance(h, int) and h == 0):
                    dve.wait_ge(sem("gq_mm"), 3 * h)
                    dve.wait_ge(sem("kq_ready"), h)
                c.mark(dve.scalar_tensor_tensor(S1[:, m, 0:SEQ], TH1[:, 0:SEQ], 1.0, CV[:, m, 0:SEQ],
                                                ALU.add, ALU.mult))
                sm = lambda a: a.rearrange("p (s u) -> p s u", s=NS)[:, :, 0:DS]
                c.tell(dve.scalar_tensor_tensor(S1[:, m, SEQ:].rearrange("p (s u) -> p s u", s=NS),
                                                sm(TH1[:, US:]), 1.0, sm(CV[:, m, US:]),
                                                ALU.add, ALU.mult), sem("s1_ready"), 3 * h + m + 1)

            def exponents(h, b):
                if b == 0:
                    dve.wait_ge(sem("rowb_in"), 16 * h + 16)
                    c.mark(dve.tensor_copy(HC, CA[:, :, :, bass.ds(h, 1)].rearrange("p q t a -> p q (t a)")))
                    c.sync()
                nb = 4 if b < 2 else 1
                for q, E in ((0, EA), (1, EQ)):
                    for i in range(nb):
                        k = 4 * b + i
                        x = dve.scalar_tensor_tensor(E[:, i], rowb[:, q, k * P:(k + 1) * P],
                                                     HC[:, 0, k:k + 1], MU[:, b // 2, q],
                                                     ALU.subtract, ALU.min)
                        if q == 0 or i < nb - 1:
                            c.mark(x)
                x.then_inc(sem("e_arg"), 1)

            def delta(h, b, ahead):
                nb = 4 if b < 2 else 1
                T = 3 * h + b
                W0 = 15 * h + 6 * b
                b4 = lambda bk: B(bk)[:, 0:nb * P].rearrange("p (a t) -> p a t", t=P)
                place = iter(range(len(PLACES[b])))

                def between():
                    p = next(place)
                    if not ahead:
                        return
                    for g in ended(b, p):
                        if g >= GB:
                            gated(h + 1, g - GB)
                    for j in range(TAPS):
                        for g in ended_before(b, p, 1 + j):
                            if g < GB:
                                conv(h + 1, g, j)
                    if b == 2 and p in (4, 7, 10):
                        silu(h + 1, (p - 4) // 3)

                if b == 0:
                    dve.wait_ge(sem("s1_ready"), 3 * h + 3)
                    if not (isinstance(h, int) and h == 0):
                        dve.wait_ge(sem("sp_out"), 16 * h)
                        dve.wait_ge(sem("y1_done"), 3 * h)
                    dve.memset(SP, 0.0).then_inc(sem("st_ready"), 1)
                else:
                    dve.wait_ge(sem("y1_done"), T)
                dve.wait_ge(sem("rk_ready"), T + 1)
                dve.tensor_tensor(KN[:, 0:nb], b4(2), bc(rk[:, 0:nb], 2, P), ALU.mult
                                  ).then_inc(sem("kn_ready"), 1)
                dve.wait_ge(sem("tv"), T + 1)
                dve.tensor_tensor(VB[:, 0:nb], b4(4), bc(HC[:, 2, 4 * b:4 * b + nb], 2, P), ALU.mult
                                  ).then_inc(sem("vb_ready"), 1)
                between()
                between()
                dve.wait_ge(sem("gq_mm"), T + 1)
                dve.wait_ge(sem("e_exp"), T + 1)
                dve.wait_ge(sem("lv_ready"), 18 * h + 7 * b + 2)
                c.mark(dve.tensor_tensor(LV[:, 0, 0:nb], b4(2), LV[:, 0, 0:nb], ALU.mult))
                c.sync()
                dve.tensor_tensor(YI[:, 0:nb], bc(ident, 1, nb), LV[:, 0, 0:nb], ALU.subtract
                                  ).then_inc(sem("y0_ready"), 1)
                dve.tensor_tensor(LV[:, 1, 0:nb], b4(2), LV[:, 1, 0:nb], ALU.mult
                                  ).then_inc(sem("lv1_ready"), 1)
                c.tell(dve.tensor_tensor(UM[:, 0:nb], b4(2), EA[:, 0:nb], ALU.mult),
                       sem("um_ready"), T + 1)
                dve.tensor_tensor(EQ[:, 0:nb], b4(3), EQ[:, 0:nb], ALU.mult
                                  ).then_inc(sem("qkt_ready"), 1)
                between()
                for lv in range(1, (6 if b < 2 else 3) + 1):
                    between()
                    dve.wait_ge(sem("n_mm"), W0 + lv)
                    dst = XI if lv < 6 else YI
                    if lv == 1:
                        dve.wait_ge(sem("xi_ready"), T + 1)
                    else:
                        dve.wait_ge(sem("n_ev1"), W0 + lv - 1)
                    if lv == 6:
                        dve.wait_ge(sem("y_ev"), 13 * h + 5 * b + 5)
                    dve.tensor_tensor(dst[:, 0:nb], dst[:, 0:nb], b4(2), ALU.subtract
                                      ).then_inc(sem("n_ev1"), 1)
                    between()
                    if lv < 6:
                        between()
                if b == 2:
                    dve.wait_ge(sem("kqs_mm"), h + 1)
                    dve.tensor_copy(KQS.rearrange("p a (s u) -> p a s u", s=NS),
                                    B(6)[:, 0:256].rearrange("p (s a u) -> p a s u", s=NS, a=2)
                                    ).then_inc(sem("kqs_ev"), 1)
                    between()
                for i in range(nb):
                    k = 4 * b + i
                    cc = 9 * h + k
                    dve.wait_ge(sem("ks_mm"), cc + 1)
                    dve.wait_ge(sem("vb_ready"), T + 1)
                    dve.scalar_tensor_tensor(RR, B(6)[:, 0:P], HC[:, 3, k:k + 1], VB[:, i],
                                             ALU.mult, ALU.add).then_inc(sem("r_ready"), 1)
                    between()
                    dve.wait_ge(sem("tr_mm"), cc + 1)
                    dve.tensor_copy(VN, B(6)[:, P:2 * P]).then_inc(sem("vn_ready"), 1)
                    between()
                    if b < 2:
                        dve.wait_ge(sem("kv_mm"), 8 * h + k + 1)
                        if k:
                            dve.wait_ge(sem("st_ready"), cc + 1)
                        dve.scalar_tensor_tensor(SP, SP, EG[:, bass.ds(h, 1), k], B(6)[:, 2 * P:3 * P],
                                                 ALU.mult, ALU.add).then_inc(sem("st_ready"), 1)
                    else:
                        dve.wait_ge(sem("vn_ready"), cc + 1)
                        dve.tensor_tensor(VM, bc(VN, 1, NS), bc(M8, 2, P), ALU.mult
                                          ).then_inc(sem("vm_ready"), 1)
                    dve.wait_ge(sem("o_mm"), cc + 1)
                    dve.tensor_tensor(OO[:, i], QE, B(7)[:, P:2 * P], ALU.add
                                      ).then_inc(sem("o_ready"), 1)
                    between()
                if b == 2:
                    dve.wait_ge(sem("skv_mm"), h + 1)
                    c.mark(dve.tensor_tensor(
                        SS1, SS1, bc(EG[:, bass.ds(h, 1), 8:16].rearrange("p a s -> p (a s)"), 2, P),
                        ALU.mult))
                    c.sync()
                    dve.tensor_tensor(SS1.rearrange("p s v -> p (s v)"), SS1.rearrange("p s v -> p (s v)"),
                                      psum[:, 4:6].rearrange("p a b -> p (a b)"), ALU.add
                                      ).then_inc(sem("ss_ready"), 1)
                dve.wait_ge(sem("o_ready"), 9 * h + 4 * b + nb)
                if b < 2:
                    exponents(h, b + 1)
                elif ahead:
                    exponents(h + 1, 0)
                dve.wait_ge(sem("fo_ready"), T + 1)
                dve.tensor_tensor(ON[:, 0:nb], OO[:, 0:nb], bc(fo[:, 0:nb], 2, P), ALU.mult
                                  ).then_inc(sem("on_ready"), 1)
                between()
                dve.wait_ge(sem("o_tp"), T + 1)
                dve.wait_ge(sem("z_ev"), 3 * h + 3)
                y = YT[:, bass.ds(h, 1), 4 * b * P:(4 * b + nb) * P].rearrange("p a t -> p (a t)")
                dve.scalar_tensor_tensor(y, B(2)[:, 0:nb * P], HN, y, ALU.mult, ALU.mult
                                         ).then_inc(sem("y1_done"), 1)
                between()
                assert not list(place)

            def head(h, ahead=True):
                for b in range(3):
                    delta(h, b, ahead)

            for g in range(GROUPS):
                if g < GB:
                    for j in range(TAPS):
                        conv(0, g, j)
                else:
                    gated(0, g - GB)
            for m in range(3):
                silu(0, m)
            exponents(0, 0)
            tiles(dve, c, H - 1, head)
            head(H - 1, False)

            def last(t, slot, turn):
                dve.wait_ge(sem(f"xt_in{slot}"), 16 * turn + 16)
                out(1, t, slot, XT[:, slot], otmp1)

            nine(dve, c, last)


def _rows(w):
    return np.ascontiguousarray(w.reshape(KT, P, -1).transpose(1, 0, 2))


def _cols(v):
    return np.ascontiguousarray(v.reshape(-1, P).T)


def _shape_constants():
    c = {"ident": np.eye(P, dtype=np.float32)}
    sel = np.zeros((9, 2, P), np.float32)
    sel[0, 0] = 1
    for s in range(NS):
        sel[1 + s, 1, s * DS:(s + 1) * DS] = 1
    c["sel"] = sel
    am = np.zeros((P, 2, 2 * WIN), np.float32)
    am[:64, :, 192:] = NEG
    am[64:, :, :64] = NEG
    am[:, 0, :WIN] = NEG
    c["amask"] = am
    sm = np.full((NS, 2 * WIN), NEG, np.float32)
    sm[:, :WIN] = 0
    for s in range(NS):
        sm[s, WIN + s * DS:WIN + (s + 1) * DS] = 0
    c["smask"] = sm.reshape(1, -1)
    pos = np.concatenate([np.arange(SEQ), np.tile(1024 + np.arange(DS), NS)]).astype(np.float32)
    inv = (500000.0 ** (-(np.arange(8, dtype=np.float32) * 2.0 / 16))).astype(np.float32)
    ang = pos[:, None] * inv[None, :]
    co, si = np.cos(ang).astype(np.float32), np.sin(ang).astype(np.float32)
    r = np.concatenate([co, co, -si, si], 1)
    c["rope"] = np.ascontiguousarray(r.reshape(NT, P, 32).transpose(1, 0, 2))
    j, i = np.arange(P)[:, None], np.arange(P)[None, :]
    mu = np.full((P, 2, 2, P), NEG, np.float32)
    for w, same in enumerate((j >= 0, j // DS == i // DS)):
        mu[:, w, 0][(i > j) & same] = 0
        mu[:, w, 1][(i >= j) & same] = 0
    c["maskU"] = mu
    lm = np.zeros((P, 7, P), np.float32)
    for lv in range(7):
        n = 1 << lv
        lm[:, lv] = (j // (2 * n) == i // (2 * n)) & ((j // n) % 2 == 0) & ((i // n) % 2 == 1)
    c["lmask"] = lm
    c["mask8"] = (np.arange(P)[:, None] // DS == np.arange(NS)[None, :]).astype(np.float32)
    r = np.ones((H, TOK), np.float32)
    r[:, 0:SEQ:P] = 0
    r[:, SEQ::DS] = 0
    c["reset"] = r
    return c


def _lay_out(a):
    d = _shape_constants()
    x = np.concatenate([a["x_prompt"].reshape(SEQ, D), a["x_sample"].reshape(P, D)])
    d["x"] = np.ascontiguousarray(x.reshape(NT, P, D).transpose(1, 0, 2))
    cc = np.concatenate([a["c_prompt"], a["c_sample"]])
    d["cT"] = np.ascontiguousarray(cc.T.reshape(KT, P, 9).transpose(1, 0, 2))
    d["modw"] = np.ascontiguousarray(np.stack([a["ev_mod_w"][0], a["od_mod_w"][0]])
                                     .reshape(2, KT, P, 6, 512).transpose(0, 3, 2, 1, 4))
    d["modb"] = np.stack([a["ev_mod_b"][0], a["od_mod_b"][0]])
    d["npre"] = np.stack([_cols(a["ev_norm_pre"][0]), _cols(a["od_norm_pre"][0])], 1)
    d["npost"] = np.stack([a["ev_norm_post"][0], a["od_norm_post"][0]])
    w = a["ev_w_in"][0]
    pair = np.concatenate([np.r_[HD * j:HD * j + HD, HD * (j + 4):HD * (j + 4) + HD] for j in range(4)])
    xa, ga, gb = w[:, 0:512], w[:, 512:1024], w[:, 1792:][:, pair]
    order = [xa[:, m * P:(m + 1) * P] for m in range(4)]
    for m in range(4):
        order += [ga[:, m * P:(m + 1) * P], gb[:, m * P:(m + 1) * P]]
    d["w0"] = np.stack([_rows(o) for o in order])
    d["wqkv"] = _rows(w[:, 1024:1792])
    wo = a["ev_w_out"][0]
    wo = np.concatenate([wo[:512], wo[512:][pair]])
    d["wout"] = np.stack([_rows(wo), _rows(a["od_w_out"][0])])
    d["cw0"] = np.ascontiguousarray(np.stack(
        [_cols(a["lru_conv_w"][0, j]) for j in range(TAPS)] + [_cols(a["lru_conv_b"][0])], 2))
    d["gbias"] = np.ascontiguousarray(np.stack([_cols(a["lru_b_a"][0]), _cols(a["lru_b_x"][0])], 2))
    d["lam"] = _cols(a["lru_lambda"][0])
    g = np.zeros((LM, P, 2, P), np.float32)
    for m in range(LM):
        for q in range(2):
            b = slice(q * 64, q * 64 + 64)
            g[m, b, 0, b] = a["lru_w_a"][0, 2 * m + q]
            g[m, b, 1, b] = a["lru_w_x"][0, 2 * m + q]
    d["gw"] = g
    ch = lambda v, n: np.ascontiguousarray(
        v.reshape(*v.shape[:-1], n, P).transpose(v.ndim, v.ndim - 1, *range(v.ndim - 1)))
    d["cs0"] = ch(a["state_lru_conv"][0], LM)
    d["h0"] = ch(a["state_lru_h"][0], LM)
    d["kc"] = np.ascontiguousarray(a["cache_swa_k"][0].reshape(NS, P, P).transpose(2, 0, 1))
    d["vc"] = np.ascontiguousarray(a["cache_swa_v"][0].reshape(NS, P, P).transpose(1, 0, 2))
    d["sinkP"] = a["swa_sinks"][0].reshape(1, 8)
    d["sinkS"] = np.repeat(a["swa_sinks"][0], DS).reshape(P, 1)
    w = a["od_w_in"][0]
    w1 = w[:, :4096].reshape(D, 4, H, P).transpose(2, 1, 0, 3).reshape(4 * H, D, P)
    d["w1"] = np.ascontiguousarray(w1.reshape(4 * H, KT, P, P).transpose(0, 2, 1, 3))
    ba = np.zeros((D, 40), np.float32)
    ba[:, 0:H], ba[:, 32:40] = w[:, 4096:4104], w[:, 4104:4112]
    d["wba"] = _rows(ba)
    d["alog"], d["dtb"] = a["gdn_a_log"].reshape(H, 1), a["gdn_dt_bias"].reshape(H, 1)
    hm = lambda v: ch(v.reshape(*v.shape[:-1], 3, H, P).swapaxes(-3, -2).reshape(*v.shape), 3 * H)
    d["cw1"] = hm(a["gdn_conv_w"][0])
    d["cs1"] = hm(a["state_gdn_conv"][0])
    d["hn"] = a["gdn_head_norm"][0].reshape(P, 1)
    d["gs"] = np.ascontiguousarray(a["state_gdn_s"][0].transpose(1, 2, 0, 3))
    return d


_OUTS = {"y": (P, NT, D), "cb0": (P, LM, 1 + NS, PRE), "hc": (P, LM, 1 + NS), "kout": (2, P, 2, HD),
         "vout": (2, P, P), "cb1": (P, 3 * H, 1 + NS, PRE), "sp": (H, P, P), "ss": (H, P, NS, P)}


def _read_out(r):
    y = r["y"].transpose(1, 0, 2).reshape(TOK, D)
    cb0 = r["cb0"].transpose(1, 0, 2, 3).reshape(LW, 1 + NS, PRE)
    hc = r["hc"].transpose(1, 0, 2).reshape(LW, 1 + NS)
    cb1 = r["cb1"].reshape(P, H, 3, 1 + NS, PRE).transpose(3, 4, 2, 1, 0).reshape(1 + NS, PRE, 3 * D)
    k, v = r["kout"], r["vout"].reshape(2, P, 2, HD)
    outs = (y[:SEQ].reshape(1, SEQ, D), y[SEQ:].reshape(NS, DS, D),
            cb0[:, 0].T.reshape(1, 1, PRE, LW), cb0[:, 1:].transpose(1, 2, 0)[None],
            hc[:, 0].reshape(1, 1, LW), hc[:, 1:].T[None],
            k[0][None, None], k[1].reshape(1, NS, DS, 2, HD),
            v[0][None, None], v[1].reshape(1, NS, DS, 2, HD),
            cb1[0][None, None], cb1[1:][None],
            r["sp"][None, None], r["ss"].transpose(2, 0, 1, 3)[None])
    return tuple(np.ascontiguousarray(o) for o in outs)


def kernel(**inputs):
    import concourse.bacc as bacc
    from concourse.bass_utils import run_bass_kernel_spmd

    nc = bacc.Bacc("TRN2", target_bir_lowering=False, num_devices=1)
    arrays = {k: np.ascontiguousarray(v) for k, v in _lay_out(inputs).items()}
    ins = {k: nc.dram_tensor(k, v.shape, F32, kind="ExternalInput").ap() for k, v in arrays.items()}
    outs = {k: nc.dram_tensor(k, shape, F32, kind="ExternalOutput").ap() for k, shape in _OUTS.items()}
    encoder(nc, ins, outs)
    r = run_bass_kernel_spmd(nc, [arrays], core_ids=[0])
    return _read_out(r.results[0])
```
